# Optimizing a Trainium2 kernel written in Bass

```python
import jax, jax.numpy as jnp
from jax import lax
import numpy as np
import math

D_MODEL = 1024
BATCH = 1
SEQ = 256
DEPTH = 2

POOL_WINDOWS = (2, 4, 8, 16)
POOL_WIDTH = 512
POOL_GROUP = POOL_WIDTH // len(POOL_WINDOWS)
N_HEADS = 8
HEAD_DIM = 64
ATTN_WIDTH = N_HEADS * HEAD_DIM
MOBA_BLOCK = 256
MOBA_TOP_K = 3
Q_CHUNK = 64
ROPE_THETA = 10000.0
N_BRANCH = 2
IN_WIDTH = POOL_WIDTH + 3 * ATTN_WIDTH + N_BRANCH * D_MODEL
D_FF = 2816
EPS = 1e-6
NEG = -1e30


def rms_norm(x, g):
    xf = x.astype(jnp.float32)
    y = xf * lax.rsqrt(jnp.mean(xf * xf, axis=-1, keepdims=True) + EPS)
    return (y * g.astype(jnp.float32)).astype(x.dtype)

def swiglu(h, w_gate_up, w_down):
    a, b = jnp.split(h @ w_gate_up, 2, axis=-1)
    return (jax.nn.silu(a) * b) @ w_down

def rope(x):
    S, Dh = x.shape[1], x.shape[-1]
    half = Dh // 2
    inv_freq = 1.0 / (ROPE_THETA ** (jnp.arange(half, dtype=jnp.float32) * (2.0 / Dh)))
    ang = jnp.arange(S, dtype=jnp.float32)[:, None] * inv_freq[None, :]
    cos = jnp.cos(ang)[None, :, None, :]
    sin = jnp.sin(ang)[None, :, None, :]
    xf = x.astype(jnp.float32)
    x1, x2 = xf[..., :half], xf[..., half:]
    out = jnp.concatenate([x1 * cos - x2 * sin, x2 * cos + x1 * sin], axis=-1)
    return out.astype(x.dtype)

def multiscale_pool(u, w_grp, scale):
    B, S, _ = u.shape
    G = len(POOL_WINDOWS)
    uf = u.astype(jnp.float32).reshape(B, S, G, POOL_GROUP)
    csum = jnp.concatenate([jnp.zeros((B, 1, G, POOL_GROUP), jnp.float32),
                            jnp.cumsum(uf, axis=1)], axis=1)
    t = jnp.arange(S)
    means = []
    for g, w in enumerate(POOL_WINDOWS):
        lo = jnp.maximum(t + 1 - w, 0)
        cnt = (t + 1 - lo).astype(jnp.float32)
        means.append((csum[:, 1:, g] - csum[:, lo, g]) / cnt[None, :, None])
    pooled = jnp.stack(means, axis=2)
    d = (pooled - uf).astype(u.dtype)
    y = jnp.einsum('bsgc,gcd->bsgd', d, w_grp).reshape(B, S, POOL_WIDTH)
    return y * scale

def moba_attention(q, k, v):
    B, S, H, Dh = q.shape
    nb = -(-S // MOBA_BLOCK)
    pad = nb * MOBA_BLOCK - S
    kp = jnp.pad(k, ((0, 0), (0, pad), (0, 0), (0, 0)))
    vp = jnp.pad(v, ((0, 0), (0, pad), (0, 0), (0, 0)))
    kb = kp.reshape(B, nb, MOBA_BLOCK, H, Dh).transpose(0, 3, 1, 2, 4)
    vb = vp.reshape(B, nb, MOBA_BLOCK, H, Dh).transpose(0, 3, 1, 2, 4)
    kbar = jnp.mean(kb.astype(jnp.float32), axis=3)
    nc = S // Q_CHUNK
    qc = q.reshape(B, nc, Q_CHUNK, H, Dh).transpose(1, 0, 3, 2, 4)
    k_eff = min(MOBA_TOP_K, nb)
    scale = Dh ** -0.5
    bi = jnp.arange(B)[:, None, None, None]
    hi = jnp.arange(H)[None, :, None, None]
    blk_ids = jnp.arange(nb)

    def one_chunk(args):
        qi, ci = args
        q0 = ci * Q_CHUNK
        qblk = q0 // MOBA_BLOCK
        qpos = q0 + jnp.arange(Q_CHUNK)
        gate = jnp.einsum('bhqd,bhnd->bhqn', qi.astype(jnp.float32), kbar)
        gate = jnp.where(blk_ids < qblk, gate, NEG)
        _, sel = lax.top_k(gate, k_eff)
        valid = sel < qblk
        ksel = kb[bi, hi, sel]
        vsel = vb[bi, hi, sel]
        kown = lax.dynamic_index_in_dim(kb, qblk, axis=2, keepdims=False)
        vown = lax.dynamic_index_in_dim(vb, qblk, axis=2, keepdims=False)
        s_sel = jnp.einsum('bhqd,bhqknd->bhqkn', qi, ksel).astype(jnp.float32) * scale
        s_sel = jnp.where(valid[..., None], s_sel, NEG).reshape(B, H, Q_CHUNK, k_eff * MOBA_BLOCK)
        kpos = qblk * MOBA_BLOCK + jnp.arange(MOBA_BLOCK)
        s_own = jnp.einsum('bhqd,bhnd->bhqn', qi, kown).astype(jnp.float32) * scale
        s_own = jnp.where(kpos[None, :] <= qpos[:, None], s_own, NEG)
        p = jax.nn.softmax(jnp.concatenate([s_sel, s_own], axis=-1), axis=-1).astype(v.dtype)
        p_sel = p[..., :k_eff * MOBA_BLOCK].reshape(B, H, Q_CHUNK, k_eff, MOBA_BLOCK)
        p_own = p[..., k_eff * MOBA_BLOCK:]
        return (jnp.einsum('bhqkn,bhqknd->bhqd', p_sel, vsel)
                + jnp.einsum('bhqn,bhnd->bhqd', p_own, vown))

    out = lax.map(one_chunk, (qc, jnp.arange(nc)))
    return out.transpose(1, 0, 3, 2, 4).reshape(B, S, H * Dh)

def hybrid_layer(x, ffn1_norm, ffn1_w_gate_up, ffn1_w_down, mix_norm, w_in, b_gate,
                 pool_w, pool_scale, q_norm, k_norm, w_branch_pool, w_branch_attn, w_out,
                 ffn2_norm, ffn2_w_gate_up, ffn2_w_down):
    B, S, D = x.shape
    x = x + 0.5 * swiglu(rms_norm(x, ffn1_norm), ffn1_w_gate_up, ffn1_w_down)
    h = rms_norm(x, mix_norm)
    z = h @ w_in
    o1 = POOL_WIDTH
    o2 = o1 + ATTN_WIDTH
    o3 = o2 + ATTN_WIDTH
    o4 = o3 + ATTN_WIDTH
    u, q, k, v, gl = z[..., :o1], z[..., o1:o2], z[..., o2:o3], z[..., o3:o4], z[..., o4:]
    y_pool = multiscale_pool(u, pool_w, pool_scale)
    q = rope(rms_norm(q.reshape(B, S, N_HEADS, HEAD_DIM), q_norm))
    k = rope(rms_norm(k.reshape(B, S, N_HEADS, HEAD_DIM), k_norm))
    v = v.reshape(B, S, N_HEADS, HEAD_DIM)
    y_attn = moba_attention(q, k, v)
    gates = jax.nn.sigmoid(gl + b_gate).reshape(B, S, N_BRANCH, D)
    merged = gates[:, :, 0] * (y_pool @ w_branch_pool) + gates[:, :, 1] * (y_attn @ w_branch_attn)
    x = x + merged @ w_out
    x = x + 0.5 * swiglu(rms_norm(x, ffn2_norm), ffn2_w_gate_up, ffn2_w_down)
    return x

def first_inputs(seed: int = 0) -> dict:
    key = jax.random.key(seed)
    ks = jax.random.split(key, 18)
    f32 = jnp.float32

    def w(k, shape, fan_in):
        return jax.random.normal(k, shape, f32) * (fan_in ** -0.5)

    def gain(k, shape):
        return 1.0 + 0.1 * jax.random.normal(k, shape, f32)

    L = DEPTH
    return {
        "x": jax.random.normal(ks[0], (BATCH, SEQ, D_MODEL), f32),
        "ffn1_norm": gain(ks[1], (L, D_MODEL)),
        "ffn1_w_gate_up": w(ks[2], (L, D_MODEL, 2 * D_FF), D_MODEL),
        "ffn1_w_down": w(ks[3], (L, D_FF, D_MODEL), D_FF),
        "mix_norm": gain(ks[4], (L, D_MODEL)),
        "w_in": w(ks[5], (L, D_MODEL, IN_WIDTH), D_MODEL),
        "b_gate": 0.1 * jax.random.normal(ks[6], (L, N_BRANCH * D_MODEL), f32),
        "pool_w": w(ks[7], (L, len(POOL_WINDOWS), POOL_GROUP, POOL_GROUP), POOL_GROUP),
        "pool_scale": gain(ks[8], (L, POOL_WIDTH)),
        "q_norm": gain(ks[9], (L, HEAD_DIM)),
        "k_norm": gain(ks[10], (L, HEAD_DIM)),
        "w_branch_pool": w(ks[11], (L, POOL_WIDTH, D_MODEL), POOL_WIDTH),
        "w_branch_attn": w(ks[12], (L, ATTN_WIDTH, D_MODEL), ATTN_WIDTH),
        "w_out": w(ks[13], (L, D_MODEL, D_MODEL), D_MODEL),
        "ffn2_norm": gain(ks[14], (L, D_MODEL)),
        "ffn2_w_gate_up": w(ks[15], (L, D_MODEL, 2 * D_FF), D_MODEL),
        "ffn2_w_down": w(ks[16], (L, D_FF, D_MODEL), D_FF),
    }

def first_block(x, ffn1_norm, ffn1_w_gate_up, ffn1_w_down, mix_norm, w_in, b_gate,
              pool_w, pool_scale, q_norm, k_norm, w_branch_pool, w_branch_attn, w_out,
              ffn2_norm, ffn2_w_gate_up, ffn2_w_down):
    for l in range(DEPTH):
        x = hybrid_layer(x, ffn1_norm[l], ffn1_w_gate_up[l], ffn1_w_down[l], mix_norm[l],
                         w_in[l], b_gate[l], pool_w[l], pool_scale[l], q_norm[l], k_norm[l],
                         w_branch_pool[l], w_branch_attn[l], w_out[l],
                         ffn2_norm[l], ffn2_w_gate_up[l], ffn2_w_down[l])
    return x


GRID_W = 64
NA_HEADS = 8
NA_HEAD_DIM = 64
NA_WIN_ROWS = 8
NA_WIN_COLS = 16
NA_W = NA_HEADS * NA_HEAD_DIM
RET_HEADS = 4
RET_QK_DIM = 128
RET_V_DIM = 256
RET_CHUNK = 128
RET_QK_W = RET_HEADS * RET_QK_DIM
RET_V_W = RET_HEADS * RET_V_DIM
ROPE_BASE = 10000.0
IN_SIZES = (NA_W, NA_W, NA_W, RET_QK_W, RET_QK_W, RET_V_W, RET_V_W, D_MODEL, D_MODEL)
IN_SPLITS = tuple(int(s) for s in np.cumsum(IN_SIZES)[:-1])
D_IN = int(sum(IN_SIZES))
CONV_W = 3
PLE_DIM = 256
LN_EPS = 1e-5
GN_EPS = 1e-6
DEEPNORM_ALPHA = (2.0 * DEPTH) ** 0.25
DEEPNORM_BETA = (8.0 * DEPTH) ** -0.25


def layer_norm(x, g, b):
    xf = x.astype(jnp.float32)
    mu = jnp.mean(xf, axis=-1, keepdims=True)
    var = jnp.mean(jnp.square(xf - mu), axis=-1, keepdims=True)
    y = (xf - mu) * lax.rsqrt(var + LN_EPS) * g.astype(jnp.float32) + b.astype(jnp.float32)
    return y.astype(x.dtype)

def rotary(x, pos):
    half = x.shape[-1] // 2
    inv = ROPE_BASE ** (-jnp.arange(half, dtype=jnp.float32) / half)
    ang = pos[:, None] * inv[None, :]
    cos, sin = jnp.cos(ang), jnp.sin(ang)
    x1, x2 = x[..., :half].astype(jnp.float32), x[..., half:].astype(jnp.float32)
    return jnp.concatenate([x1 * cos - x2 * sin, x2 * cos + x1 * sin], axis=-1).astype(x.dtype)

def neighbourhood_attention(q, k, v, rpb):
    B, T, H, dh = q.shape
    rows = T // GRID_W
    wr = min(NA_WIN_ROWS, rows)
    scale = dh ** -0.5
    q_g = q.reshape(B, rows, GRID_W, H, dh).transpose(1, 0, 3, 2, 4)
    k_g = k.reshape(B, rows, GRID_W, H, dh).transpose(0, 3, 1, 2, 4)
    v_g = v.reshape(B, rows, GRID_W, H, dh).transpose(0, 3, 1, 2, 4)
    cols = np.arange(GRID_W)
    col_start = np.clip(cols - NA_WIN_COLS // 2, 0, GRID_W - NA_WIN_COLS)
    col_idx = col_start[:, None] + np.arange(NA_WIN_COLS)[None, :]
    col_off = col_idx - cols[:, None] + (NA_WIN_COLS - 1)

    def row_step(args):
        r, q_row = args
        rs = jnp.clip(r - wr // 2, 0, rows - wr)
        k_rows = lax.dynamic_slice_in_dim(k_g, rs, wr, axis=2)
        v_rows = lax.dynamic_slice_in_dim(v_g, rs, wr, axis=2)
        k_win = jnp.take(k_rows, col_idx, axis=3)
        v_win = jnp.take(v_rows, col_idx, axis=3)
        s = jnp.einsum('bhcd,bhrckd->bhcrk', q_row, k_win).astype(jnp.float32) * scale
        row_off = rs + jnp.arange(wr) - r + (NA_WIN_ROWS - 1)
        bias = jnp.take(rpb[:, row_off], col_off, axis=2)
        s = s + bias.transpose(0, 2, 1, 3)[None].astype(jnp.float32)
        pr = jax.nn.softmax(s.reshape(B, H, GRID_W, wr * NA_WIN_COLS), axis=-1)
        pr = pr.reshape(B, H, GRID_W, wr, NA_WIN_COLS).astype(v.dtype)
        return jnp.einsum('bhcrk,bhrckd->bhcd', pr, v_win)

    out = lax.map(row_step, (jnp.arange(rows), q_g))
    return out.transpose(1, 0, 3, 2, 4).reshape(B, T, H * dh)

def retention_dir(q, k, v, gamma, include_diag):
    B, H, T, dk = q.shape
    dv = v.shape[-1]
    C = RET_CHUNK
    n = T // C
    qc = q.reshape(B, H, n, C, dk)
    kc = k.reshape(B, H, n, C, dk)
    vc = v.reshape(B, H, n, C, dv)
    log_g = jnp.log(gamma)
    i = np.arange(C)
    diff = i[:, None] - i[None, :]
    mask = (diff >= 0) if include_diag else (diff > 0)
    dpos = np.maximum(diff, 0).astype(np.float32)
    decay_in = jnp.where(mask[None], jnp.exp(log_g[:, None, None] * dpos[None]), 0.0)
    s = jnp.einsum('bhnid,bhnjd->bhnij', qc, kc) * decay_in[None, :, None]
    inner = jnp.einsum('bhnij,bhnje->bhnie', s, vc)
    zeta = jnp.exp(log_g[:, None] * (C - 1 - i).astype(np.float32))
    xi = jnp.exp(log_g[:, None] * (i + 1).astype(np.float32))
    chunk_decay = jnp.exp(log_g * C)
    kv = jnp.einsum('bhnjd,bhnje->nbhde', kc * zeta[None, :, None, :, None], vc)

    def body(S, kv_c):
        return S * chunk_decay[None, :, None, None] + kv_c, S

    S0 = jnp.zeros((B, H, dk, dv), kv.dtype)
    _, S_prev = lax.scan(body, S0, kv)
    cross = jnp.einsum('bhnid,nbhde->bhnie', qc, S_prev) * xi[None, :, None, :, None]
    return (inner + cross).reshape(B, H, T, dv)

def bidirectional_retention(q, k, v, g, decay_f, decay_b):
    B, T, H, dk = q.shape
    pos = jnp.arange(T, dtype=jnp.float32)
    qh = rotary(q.transpose(0, 2, 1, 3), pos)
    kh = rotary(k.transpose(0, 2, 1, 3), pos) * (dk ** -0.5)
    vh = v.reshape(B, T, H, RET_V_DIM).transpose(0, 2, 1, 3)
    gam_f = jax.nn.sigmoid(decay_f.astype(jnp.float32))
    gam_b = jax.nn.sigmoid(decay_b.astype(jnp.float32))
    fwd = retention_dir(qh, kh, vh, gam_f, True)
    bwd = jnp.flip(retention_dir(jnp.flip(qh, 2), jnp.flip(kh, 2), jnp.flip(vh, 2), gam_b, False), 2)
    o = (fwd + bwd).astype(jnp.float32)
    mu = jnp.mean(o, axis=-1, keepdims=True)
    var = jnp.mean(jnp.square(o - mu), axis=-1, keepdims=True)
    o = ((o - mu) * lax.rsqrt(var + GN_EPS)).astype(v.dtype)
    o = o.transpose(0, 2, 1, 3).reshape(B, T, H * RET_V_DIM)
    return jax.nn.silu(g) * o

def conv_glu_ffn(x, w_up, conv_w, conv_b, w_down):
    h = x @ w_up
    hp = jnp.pad(h, ((0, 0), (1, 1), (0, 0)))
    h = hp[:, :-2] * conv_w[0] + hp[:, 1:-1] * conv_w[1] + hp[:, 2:] * conv_w[2] + conv_b
    a, b = jnp.split(h, 2, axis=-1)
    return (jax.nn.gelu(a) * b) @ w_down

def second_inputs(seed: int = 0) -> dict:
    key = jax.random.key(seed)
    ks = jax.random.split(key, 20)
    f32 = jnp.float32
    nrm = lambda k, shape: jax.random.normal(k, shape, f32)
    beta = DEEPNORM_BETA
    col_scale = np.ones((D_IN,), np.float32)
    col_scale[2 * NA_W:3 * NA_W] = beta
    v0 = 3 * NA_W + 2 * RET_QK_W
    col_scale[v0:v0 + RET_V_W] = beta
    gam = 1.0 - 2.0 ** (-5.0 - np.arange(RET_HEADS))
    base_logit = jnp.asarray(np.log(gam / (1.0 - gam)), f32)
    return {
        "x": nrm(ks[0], (BATCH, SEQ, D_MODEL)),
        "p": nrm(ks[1], (DEPTH, BATCH, SEQ, PLE_DIM)),
        "w_in": nrm(ks[2], (DEPTH, D_MODEL, D_IN)) * (D_MODEL ** -0.5) * jnp.asarray(col_scale),
        "na_rpb": 0.02 * nrm(ks[3], (DEPTH, NA_HEADS, 2 * NA_WIN_ROWS - 1, 2 * NA_WIN_COLS - 1)),
        "ret_decay_f": base_logit + 0.01 * nrm(ks[4], (DEPTH, RET_HEADS)),
        "ret_decay_b": base_logit + 0.01 * nrm(ks[5], (DEPTH, RET_HEADS)),
        "w_branch_a": nrm(ks[6], (DEPTH, NA_W, D_MODEL)) * (NA_W ** -0.5) * beta,
        "w_branch_b": nrm(ks[7], (DEPTH, RET_V_W, D_MODEL)) * (RET_V_W ** -0.5) * beta,
        "w_out": nrm(ks[8], (DEPTH, D_MODEL, D_MODEL)) * (D_MODEL ** -0.5) * beta,
        "ln1_g": 1.0 + 0.02 * nrm(ks[9], (DEPTH, D_MODEL)),
        "ln1_b": 0.02 * nrm(ks[10], (DEPTH, D_MODEL)),
        "w_up": nrm(ks[11], (DEPTH, D_MODEL, 2 * D_FF)) * (D_MODEL ** -0.5) * beta,
        "conv_w": nrm(ks[12], (DEPTH, CONV_W, 2 * D_FF)) * (CONV_W ** -0.5),
        "conv_b": 0.02 * nrm(ks[13], (DEPTH, 2 * D_FF)),
        "w_down": nrm(ks[14], (DEPTH, D_FF, D_MODEL)) * (D_FF ** -0.5) * beta,
        "w_ple_gate": nrm(ks[15], (DEPTH, D_MODEL, D_MODEL)) * (D_MODEL ** -0.5),
        "w_ple_proj": nrm(ks[16], (DEPTH, PLE_DIM, D_MODEL)) * (PLE_DIM ** -0.5) * beta,
        "ln2_g": 1.0 + 0.02 * nrm(ks[17], (DEPTH, D_MODEL)),
        "ln2_b": 0.02 * nrm(ks[18], (DEPTH, D_MODEL)),
    }

def second_block(x, p, w_in, na_rpb, ret_decay_f, ret_decay_b, w_branch_a, w_branch_b, w_out,
              ln1_g, ln1_b, w_up, conv_w, conv_b, w_down, w_ple_gate, w_ple_proj, ln2_g, ln2_b):
    B, T, _ = x.shape
    for i in range(DEPTH):
        proj = x @ w_in[i]
        q_na, k_na, v_na, q_r, k_r, v_r, g_r, gate_a, gate_b = jnp.split(proj, IN_SPLITS, axis=-1)
        ya = neighbourhood_attention(q_na.reshape(B, T, NA_HEADS, NA_HEAD_DIM),
                                     k_na.reshape(B, T, NA_HEADS, NA_HEAD_DIM),
                                     v_na.reshape(B, T, NA_HEADS, NA_HEAD_DIM), na_rpb[i])
        yb = bidirectional_retention(q_r.reshape(B, T, RET_HEADS, RET_QK_DIM),
                                     k_r.reshape(B, T, RET_HEADS, RET_QK_DIM),
                                     v_r, g_r, ret_decay_f[i], ret_decay_b[i])
        merged = jax.nn.sigmoid(gate_a) * (ya @ w_branch_a[i]) + jax.nn.sigmoid(gate_b) * (yb @ w_branch_b[i])
        y = merged @ w_out[i]
        x = layer_norm(DEEPNORM_ALPHA * x + y, ln1_g[i], ln1_b[i])
        ffn = conv_glu_ffn(x, w_up[i], conv_w[i], conv_b[i], w_down[i])
        ple = jax.nn.sigmoid(x @ w_ple_gate[i]) * (p[i] @ w_ple_proj[i])
        x = layer_norm(DEEPNORM_ALPHA * x + ffn + ple, ln2_g[i], ln2_b[i])
    return x


def setup_inputs(seed=0):
    out = dict(first_inputs(seed))
    for name, value in second_inputs(seed + 1).items():
        if name != "x":
            out[name + "_2"] = value
    return out


def reference(
    x, ffn1_norm, ffn1_w_gate_up, ffn1_w_down, mix_norm, w_in, b_gate, pool_w, pool_scale,
    q_norm, k_norm, w_branch_pool, w_branch_attn, w_out, ffn2_norm, ffn2_w_gate_up, ffn2_w_down,
    p_2, w_in_2, na_rpb_2, ret_decay_f_2, ret_decay_b_2, w_branch_a_2, w_branch_b_2, w_out_2,
    ln1_g_2, ln1_b_2, w_up_2, conv_w_2, conv_b_2, w_down_2, w_ple_gate_2, w_ple_proj_2, ln2_g_2,
    ln2_b_2,
):
    x = first_block(
        x, ffn1_norm, ffn1_w_gate_up, ffn1_w_down, mix_norm, w_in, b_gate, pool_w, pool_scale,
        q_norm, k_norm, w_branch_pool, w_branch_attn, w_out, ffn2_norm, ffn2_w_gate_up,
        ffn2_w_down,
    )
    return second_block(
        x, p_2, w_in_2, na_rpb_2, ret_decay_f_2, ret_decay_b_2, w_branch_a_2, w_branch_b_2,
        w_out_2, ln1_g_2, ln1_b_2, w_up_2, conv_w_2, conv_b_2, w_down_2, w_ple_gate_2,
        w_ple_proj_2, ln2_g_2, ln2_b_2,
    )


_drawn_inputs = setup_inputs


def setup_inputs(seed=0):
    import zlib

    import numpy as np

    out = dict(_drawn_inputs(seed))
    spreads = {}
    factors = {'q_norm': 4.513,
     'k_norm': 4.336,
     'na_rpb_2': 59.161,
     'ret_decay_f_2': 24.512,
     'ret_decay_b_2': 24.624,
     'w_branch_a_2': 2.713,
     'conv_b_2': 8.0}
    for name, (base, spread) in spreads.items():
        noise = np.random.default_rng([zlib.crc32(name.encode()), seed]).standard_normal(out[name].shape)
        drawn = base * np.exp(spread * noise) if base else spread * noise
        out[name] = __import__('jax').numpy.asarray(drawn.astype(out[name].dtype))
    for name, factor in factors.items():
        out[name] = (out[name] * factor).astype(out[name].dtype)
    return out
```

```python
from contextlib import ExitStack

import numpy as np

import concourse.bass as bass
from concourse import mybir

F32 = mybir.dt.float32
F32R = mybir.dt.float32r
ACT = mybir.ActivationFunctionType
ALU = mybir.AluOpType
AX_X = mybir.AxisListType.X

P = 128
T = 256
D = 1024
DT = D // P
TT = T // P
DEPTH = 2
D_FF = 2816
PAIRS = D_FF // T
HEADS, HEAD_DIM = 8, 64
HALVES = HEADS // 2
WINDOWS = (2, 4, 8, 16)
POOL_EDGE = max(WINDOWS)
RET_HEADS, RET_QK, RET_V = 4, 128, 256
GRID_W, NA_ROWS, NA_COLS = 64, 8, 16
GRID_ROWS = T // GRID_W
ROW_STEPS = GRID_ROWS + P // GRID_W
PLE = 256
ROPE_BASE = 10000.0
EPS, LN_EPS, GN_EPS = 1e-6, 1e-5, 1e-6
ALPHA = (2.0 * DEPTH) ** 0.25
NEG = -1e30

SLOTS = 3
CHUNK = 2048
FFN_CHUNKS = 3 * PAIRS
MIX1 = 24
MIX2 = 42
CHUNKS = (2 * FFN_CHUNKS + MIX1, MIX2 + FFN_CHUNKS)
USES = tuple(c // SLOTS for c in CHUNKS)
STREAM = DEPTH * sum(CHUNKS)

C_FFN1, C_MIX, C_FFN2, C_GATE, C_SCALE, C_Q, C_K = 0, 8, 16, 24, 40, 44, 45
COLS1 = 46
FT = 2 * D_FF // P
C_G1, C_B1, C_G2, C_B2, C_TAP, C_CONVB = 0, 8, 16, 24, 32, 32 + 3 * FT
C_LF = C_CONVB + FT
C_LB = C_LF + RET_HEADS
COLS2 = C_LB + RET_HEADS

K_IDENT, K_MEAN, K_HEAD, K_ROT1, K_ROT2 = 0, P, 2 * P, 3 * P, 4 * P
K_COS1 = 5 * P
K_SIN1, K_COS2, K_SIN2 = K_COS1 + T, K_COS1 + 2 * T, K_COS1 + 3 * T
K_CAUSAL = K_COS1 + 4 * T
K_DIST = K_CAUSAL + TT * T
K_WIN = K_DIST + TT * T
K_EDGE = K_WIN + GRID_W
CONSTS = K_EDGE + len(WINDOWS) * POOL_EDGE


class Signal:

    def __init__(self, sem, hybrid, second=0, setup=0, between=0):
        self.sem = sem
        self.per = (hybrid, second)
        self.before = (setup, setup + DEPTH * hybrid + between)


class Place:

    def __init__(self, kind, layer):
        self.kind, self.layer = kind, layer

    def at(self, signal, n):
        return self.layer * signal.per[self.kind] + (signal.before[self.kind] + n)

    def uses(self, c, turn=0):
        return self.layer * USES[self.kind] + (self.kind * DEPTH * USES[0] + c // SLOTS) + turn


def ffn_walk(eng, c0, step):
    for n, (kind, i) in enumerate((("A", 0), ("B", 0), ("A", 1), ("B", 1), ("D", 0))):
        step(kind, i, c0 + n, 0)
    with eng.Fori(0, PAIRS - 3) as turn:
        for n, (kind, lag) in enumerate((("A", 0), ("B", 0), ("D", 1))):
            step(kind, turn + (2 - lag), c0 + 5 + n, turn)
    for n, (kind, lag) in enumerate((("A", 0), ("B", 0), ("D", 1))):
        step(kind, PAIRS - 1 - lag, c0 + FFN_CHUNKS - 4 + n, 0)
    step("D", PAIRS - 1, c0 + FFN_CHUNKS - 1, 0)


def hybrid_and_neighbourhood_kernel(nc, xT, stream, cols1, cols2, pool_w, pT, rpb, consts, out):
    ctx = ExitStack()
    with ctx:
        def sb(name, shape, dt=F32):
            return ctx.enter_context(nc.sbuf_tensor(name, shape, dt))

        def sem(name):
            return ctx.enter_context(nc.semaphore(name))

        def signal(name, hybrid, second=0, setup=0, between=0):
            return Signal(sem(name), hybrid, second, setup, between)

        raw = sb("raw", [P, SLOTS, CHUNK])
        w_hi = sb("w_hi", [P, SLOTS, CHUNK], F32R)
        w_lo = sb("w_lo", [P, SLOTS, CHUNK], F32R)
        x = sb("x", [P, DT, T])
        in_hi = sb("in_hi", [P, DT, T], F32R)
        in_lo = sb("in_lo", [P, DT, T], F32R)
        att_hi = sb("att_hi", [P, HALVES, T], F32R)
        att_lo = sb("att_lo", [P, HALVES, T], F32R)
        br_hi = sb("br_hi", [P, DT, T], F32R)
        br_lo = sb("br_lo", [P, DT, T], F32R)
        hid_hi = sb("hid_hi", [P, 2, T], F32R)
        hid_lo = sb("hid_lo", [P, 2, T], F32R)
        ple_hi = sb("ple_hi", [P, 2, T], F32R)
        ple_lo = sb("ple_lo", [P, 2, T], F32R)
        konst = sb("konst", [P, CONSTS])
        col1 = sb("col1", [P, DEPTH, COLS1])
        col2 = sb("col2", [P, DEPTH, COLS2])
        cur = sb("cur", [P, COLS2])
        small = sb("small", [P, 8])
        eps6, eps5, minus_half = small[:, 0:1], small[:, 1:2], small[:, 2:3]
        decay = sb("decay", [P, 4, DEPTH * 2 * RET_HEADS])
        rstd = sb("rstd", [P, T])
        spread = sb("spread", [P, T])
        tmp = sb("tmp", [P, 2 * T])
        stat = sb("stat", [P, 2, 8])
        group = sb("group", [P, 2, TT, 12])
        soft = sb("soft", [P, 2, TT, T])
        softT = sb("softT", [P, 2, TT, T])
        ple_in = sb("ple_in", [P, 2, T])

        area0 = sb("area0", [P, DT, T])
        area1 = sb("area1", [P, TT, 2 * T])
        area2 = sb("area2", [P, DT, T])
        area3 = sb("area3", [P, DT, T])
        area4 = sb("area4", [P, HEADS * ROW_STEPS * GRID_W])
        area5 = sb("area5", [P, DT, T])
        work = area0
        qk = area0
        v_tok = area1
        gates1 = area2
        gates2 = area0
        merged1, merged2 = area3, area2
        glu_a = area2[:, 0:2, :]
        glu_b = area2[:, 2:4, :]
        hidden = area2[:, 4:6, :]
        u = area4[:, 0:4 * T].rearrange("p (g t) -> p g t", g=4)
        sums = [area4[:, (1 + b) * 4 * T:(2 + b) * 4 * T].rearrange("p (g t) -> p g t", g=4) for b in (0, 1)]
        pool_both = area5[:, 0:4, :].rearrange("p a t -> p (a t)")
        pool_cur = area5[:, 4:6, :].rearrange("p a t -> p (a t)")
        qk_sq = area3[:, 0:4, :].rearrange("p (b a) t -> p b (a t)", b=2)
        bias = area4[:, :].rearrange("p (h r c) -> p h r c", h=HEADS, r=ROW_STEPS)
        silu_g = area4[:, 0:DT * T].rearrange("p (f t) -> p f t", f=DT)
        ret_qk = area2
        ret_v = area3[:, :, :].rearrange("p f t -> p (f t)").rearrange("p (a n) -> p a n", a=TT)
        ret_turn = ret_v[:, :, 3 * T:4 * T]
        ple_out = area3
        ple_gate = area1
        backward = area3[:, :, :].rearrange("p (h m) t -> p h (m t)", h=RET_HEADS)
        decays = area5[:, :, :].rearrange("p (h m) t -> p h (m t)", h=RET_HEADS)

        banks = [ctx.enter_context(nc.psum_tensor(f"bank{b}", [P, 2, T], F32)) for b in range(8)]

        def flat(ap):
            return ap.rearrange("p a t -> p (a t)")

        ident = konst[:, K_IDENT:K_IDENT + P]
        mean_of = konst[:, K_MEAN:K_MEAN + P]
        head_mean = konst[:, K_HEAD:K_HEAD + P]
        rot1 = konst[:, K_ROT1:K_ROT1 + P]
        rot2 = konst[:, K_ROT2:K_ROT2 + P]

        def table(k):
            return konst[:, k:k + T].unsqueeze(1).broadcast_to([P, 2, T])

        causal = konst[:, K_CAUSAL:K_CAUSAL + TT * T].rearrange("p (a t) -> p a t", a=TT)
        dist = konst[:, K_DIST:K_DIST + TT * T]
        window = konst[:, K_WIN:K_WIN + GRID_W]
        edge = konst[:, K_EDGE:CONSTS].rearrange("p (g t) -> p g t", g=len(WINDOWS))

        raw_full = [sem(f"raw_full{s}") for s in range(SLOTS)]
        hi_ready = [sem(f"hi_ready{s}") for s in range(SLOTS)]
        lo_ready = [sem(f"lo_ready{s}") for s in range(SLOTS)]
        w_used = [sem(f"w_used{s}") for s in range(SLOTS)]
        x_in, konst_in, col_in = sem("x_in"), sem("konst_in"), sem("col_in")
        small_set = sem("small_set")
        out_done = sem("out_done")
        decay_step, decay_scal = sem("decay_step"), sem("decay_scal")
        cur_ready = signal("cur_ready", 1, 1)
        x_ready = signal("x_ready", 3 * HALVES)
        sq_ready = signal("sq_ready", 3 * HALVES, setup=HALVES)
        ss_ready = signal("ss_ready", 3, setup=1)
        sd_ready = signal("sd_ready", 3)
        rstd_ready = signal("rstd_ready", 3)
        xnf_ready = signal("xnf_ready", 3 * DT)
        xn_hi = signal("xn_hi", 3 * DT)
        xn_ready = signal("xn_ready", 3 * DT)
        gate_act = signal("gate_act", 2 * PAIRS, PAIRS)
        gate_left = signal("gate_left", 0, PAIRS)
        gate_taps = signal("gate_taps", 0, PAIRS)
        gelu_ready = signal("gelu_ready", 0, PAIRS)
        up_mid = signal("up_mid", 0, PAIRS)
        up_left = signal("up_left", 0, PAIRS)
        up_taps = signal("up_taps", 0, PAIRS)
        prod_ready = signal("prod_ready", 2 * PAIRS, PAIRS)
        hid_hi_ready = signal("hid_hi_ready", 2 * PAIRS, PAIRS)
        hid_ready = signal("hid_ready", 2 * PAIRS, PAIRS)
        acc_done = signal("acc_done", 2 * (HALVES - 1), HALVES - 1)
        mix_evac = signal("mix_evac", 16, 32)
        branch_evac = signal("branch_evac", 4, 6)
        qk_sq_ready = signal("qk_sq_ready", 4)
        qk_ms = signal("qk_ms", 4)
        qk_sd = signal("qk_sd", 4)
        qk_rstd = signal("qk_rstd", 4)
        qk_normed = signal("qk_normed", 4)
        qk_rot = signal("qk_rot", 4, 4)
        qk_sin = signal("qk_sin", 4, 4)
        qk_cos = signal("qk_cos", 4, 4)
        qk_ready = signal("qk_ready", 4, 4)
        pool_step = signal("pool_step", 14)
        pool_d = signal("pool_d", len(WINDOWS))
        pool_w_ready = signal("pool_w_ready", 1)
        pool_in = sem("pool_in")
        pool_y = signal("pool_y", 1)
        pool_hi = signal("pool_hi", 4)
        pool_ready = signal("pool_ready", 1)
        sig_ready = signal("sig_ready", 2)
        part_ready = signal("part_ready", 4, 8)
        merged_ready = signal("merged_ready", 4, 4)
        merged_hi = signal("merged_hi", 4, 4)
        merged_lo = signal("merged_lo", 4, 4)
        scored = signal("scored", HEADS, HEADS)
        masked = signal("masked", HEADS, HEADS)
        max_ready = signal("max_ready", HEADS, HEADS)
        nmax_ready = signal("nmax_ready", HEADS, HEADS)
        exp_ready = signal("exp_ready", HEADS, HEADS)
        inv_ready = signal("inv_ready", HEADS, HEADS)
        p_ready = signal("p_ready", HEADS, HEADS)
        p_turned = signal("p_turned", HEADS, HEADS)
        pT_ready = signal("pT_ready", HEADS, HEADS)
        pv_done = signal("pv_done", HEADS, HEADS)
        att_hi_ready = signal("att_hi_ready", HALVES, HALVES)
        att_ready = signal("att_ready", HALVES, HALVES)
        xs_hi = signal("xs_hi", 0, 2 * DT, between=DT)
        xs_ready = signal("xs_ready", 0, 2 * DT, between=DT)
        bias_in = sem("bias_in")
        ple_in_sem = sem("ple_in_sem")
        bias_ready = signal("bias_ready", 0, 1)
        dist_step = signal("dist_step", 0, 2 * RET_HEADS)
        dist_ready = signal("dist_ready", 0, RET_HEADS)
        decay_ready = signal("decay_ready", 0, RET_HEADS)
        ret_scored = signal("ret_scored", 0, RET_HEADS)
        ret_p = signal("ret_p", 0, RET_HEADS)
        ret_pv = signal("ret_pv", 0, RET_HEADS)
        ret_stats = signal("ret_stats", 0, RET_HEADS)
        ret_mv = signal("ret_mv", 0, RET_HEADS)
        ret_var = signal("ret_var", 0, RET_HEADS)
        ret_rstd = signal("ret_rstd", 0, RET_HEADS)
        ret_o = signal("ret_o", 0, RET_HEADS)
        ret_turned = signal("ret_turned", 0, RET_HEADS)
        ret_y = signal("ret_y", 0, RET_HEADS)
        ret_hi = signal("ret_hi", 0, RET_HEADS)
        ret_ready = signal("ret_ready", 0, RET_HEADS)
        ple_split_hi = signal("ple_split_hi", 0, 1)
        ple_split = signal("ple_split", 0, 1)
        ple_mul = signal("ple_mul", 0, 4)
        base_ready = signal("base_ready", 0, 4)
        z_ready = signal("z_ready", 0, 2 * HALVES)
        mu_ready = signal("mu_ready", 0, 2)
        c_ready = signal("c_ready", 0, 2 * DT)
        c_sq = signal("c_sq", 0, 2 * DT)
        var_ready = signal("var_ready", 0, 2)
        ln_sd = signal("ln_sd", 0, 2)
        ln_rstd = signal("ln_rstd", 0, 2)
        ln_scaled = signal("ln_scaled", 0, 2 * DT)
        x_new = signal("x_new", 0, 2 * DT)

        block = ctx.enter_context(nc.Block())

        @block.sync
        def _(sp):
            for s in range(SLOTS):
                sp.dma_start(raw[:, s, :], stream[s]).then_inc(raw_full[s], 16)
            with sp.Fori(1, STREAM // SLOTS) as n:
                for s in range(SLOTS):
                    sp.wait_ge(lo_ready[s], n)
                    sp.dma_start(raw[:, s, :], stream[bass.ds(n * SLOTS + s, 1)].rearrange("a p n -> (a p) n")
                                 ).then_inc(raw_full[s], 16)
            sp.wait_ge(x_new.sem, DEPTH * 2 * DT)
            sp.dma_start(out, flat(x[:, :, :])).then_inc(out_done, 16)
            sp.wait_ge(out_done, 16)

        @block.gpsimd
        def _(pool):
            pool.memset(eps6, EPS).then_inc(small_set, 1)
            pool.memset(eps5, LN_EPS).then_inc(small_set, 1)
            pool.memset(minus_half, -0.5).then_inc(small_set, 1)
            for g, w in enumerate(WINDOWS):
                pool.memset(small[:, 3 + g:4 + g], 1.0 / w).then_inc(small_set, 1)
            pool.wait_ge(small_set, 3 + len(WINDOWS))
            pool.dma_start(pool_both, pool_w).then_inc(pool_in, 16)
            pool.wait_ge(konst_in, 16)
            pool.wait_ge(pool_in, 16)
            with pool.Fori(0, DEPTH) as layer:
                here = Place(0, layer)
                pool.wait_ge(mix_evac.sem, here.at(mix_evac, 8))
                for k in range(len(WINDOWS)):
                    back = 2 ** k
                    src = u if k == 0 else sums[(k - 1) % 2]
                    if k:
                        pool.wait_ge(pool_step.sem, here.at(pool_step, 2 * k))
                    pool.tensor_tensor(sums[k % 2][:, k:4, back:T], src[:, k:4, back:T], src[:, k:4, 0:T - back],
                                       ALU.add).then_inc(pool_step.sem, 1)
                    pool.tensor_copy(sums[k % 2][:, k:4, 0:back], src[:, k:4, 0:back]).then_inc(pool_step.sem, 1)
                pool.tensor_copy(pool_cur, pool_both[:, bass.ds(layer * (4 * P), 4 * P)]).then_inc(pool_w_ready.sem, 1)
                pool.wait_ge(pool_step.sem, here.at(pool_step, 8))
                for b in range(2):
                    first = sums[b][:, b:4:2, 0:POOL_EDGE]
                    pool.tensor_tensor(first, first, edge[:, b:4:2, :], ALU.mult).then_inc(pool_step.sem, 1)
                pool.wait_ge(pool_step.sem, here.at(pool_step, 10))
                for g in range(len(WINDOWS)):
                    pool.tensor_tensor(sums[g % 2][:, g, :], sums[g % 2][:, g, :],
                                       small[:, 3 + g:4 + g].broadcast_to([P, T]), ALU.mult).then_inc(pool_step.sem, 1)
                for g in range(len(WINDOWS)):
                    pool.wait_ge(pool_step.sem, here.at(pool_step, 11 + g))
                    pool.tensor_tensor(sums[g % 2][:, g, :], sums[g % 2][:, g, :], u[:, g, :], ALU.subtract
                                       ).then_inc(pool_d.sem, 1)
            with pool.Fori(0, DEPTH) as layer:
                here = Place(1, layer)
                pool.wait_ge(xs_ready.sem, here.at(xs_ready, 0))
                pool.dma_start(area4[:, :], rpb[bass.ds(layer, 1)].rearrange("a p n -> (a p) n")).then_inc(bias_in, 16)
                pool.dma_start(flat(ple_in[:, :, :]), pT[bass.ds(layer, 1)].rearrange("a p n -> (a p) n")
                               ).then_inc(ple_in_sem, 16)
                pool.wait_ge(cur_ready.sem, here.at(cur_ready, 1))
                pool.wait_ge(bias_in, (layer + 1) * 16)
                masks = window.unsqueeze(1).broadcast_to([P, HEADS * ROW_STEPS, GRID_W])
                rows = area4[:, :].rearrange("p (m c) -> p m c", c=GRID_W)
                pool.tensor_tensor(rows, rows, masks, ALU.add).then_inc(bias_ready.sem, 1)
                for h in range(RET_HEADS):
                    pool.tensor_scalar(decays[:, h, :], dist, 0.0, cur[:, C_LF + h:C_LF + h + 1], ALU.max, ALU.mult
                                       ).then_inc(dist_step.sem, 1)
                    pool.tensor_scalar(backward[:, h, :], dist, 0.0, cur[:, C_LB + h:C_LB + h + 1], ALU.min, ALU.mult
                                       ).then_inc(dist_step.sem, 1)
                pool.wait_ge(dist_step.sem, here.at(dist_step, 2 * RET_HEADS))
                for h in range(RET_HEADS):
                    pool.tensor_tensor(decays[:, h, :], decays[:, h, :], backward[:, h, :], ALU.add
                                       ).then_inc(dist_ready.sem, 1)
                for h in range(RET_HEADS):
                    pool.wait_ge(ret_var.sem, here.at(ret_var, h + 1))
                    pool.tensor_tensor(group[:, h % 2, :, 11:12], group[:, h % 2, :, 10:11],
                                       minus_half.unsqueeze(1).broadcast_to([P, TT, 1]), ALU.pow
                                       ).then_inc(ret_rstd.sem, 1)

        @block.scalar
        def _(act):
            act.dma_start(flat(x[:, :, :]), xT).then_inc(x_in, 16)
            act.dma_start(konst[:, :], consts).then_inc(konst_in, 16)
            act.dma_start(col1[:, :, :].rearrange("p l c -> p (l c)"), cols1).then_inc(col_in, 16)
            act.dma_start(col2[:, :, :].rearrange("p l c -> p (l c)"), cols2).then_inc(col_in, 16)

            def split_hi(s, uses):
                act.wait_ge(raw_full[s], (uses + 1) * 16)
                act.activation(w_hi[:, s, :], raw[:, s, :], ACT.Copy).then_inc(hi_ready[s], 1)

            def chunk_done(here, c, turn=0):
                act.wait_ge(w_used[c % SLOTS], here.uses(c, turn) + 1)

            def split_after(here, c, turn=0):
                split_hi(c % SLOTS, here.uses(c, turn) + 1)

            def squares(here, stage, pairs):
                for j in pairs:
                    act.wait_ge(x_ready.sem, here.at(x_ready, HALVES * stage + j + 1))
                    act.activation(work[:, 2 * j:2 * j + 2, :], x[:, 2 * j:2 * j + 2, :], ACT.Square
                                   ).then_inc(sq_ready.sem, 1)

            def norm(here, n):
                act.wait_ge(ss_ready.sem, here.at(ss_ready, n))
                act.activation(spread[:, :], banks[6][:, 0, :], ACT.Sqrt, bias=eps6).then_inc(sd_ready.sem, 1)
                for k in range(DT):
                    act.wait_ge(xnf_ready.sem, here.at(xnf_ready, DT * n + k + 1))
                    act.activation(in_hi[:, k, :], work[:, k, :], ACT.Copy).then_inc(xn_hi.sem, 1)

            def hidden_upper(here, n):
                act.wait_ge(prod_ready.sem, here.at(prod_ready, n + 1))
                act.activation(hid_hi[:, :, :], hidden, ACT.Copy).then_inc(hid_hi_ready.sem, 1)

            def ffn(here, c0, f):
                def step(kind, i, c, turn):
                    final = c == c0 + FFN_CHUNKS - 1
                    if not final:
                        chunk_done(here, c, turn)
                    if kind == "A":
                        act.activation(glu_a, banks[4][:, :, :], ACT.Silu).then_inc(gate_act.sem, 1)
                    if kind == "B" and c == c0 + 1:
                        hidden_upper(here, f * PAIRS)
                    if kind == "D" and not final:
                        hidden_upper(here, i + (f * PAIRS + 1))
                    if not final:
                        split_after(here, c, turn)
                ffn_walk(act, c0, step)

            def softmax_exp(here, h):
                act.wait_ge(nmax_ready.sem, here.at(nmax_ready, h + 1))
                b = h % 2
                for a in range(TT):
                    e = act.activation(soft[:, b, a, :], soft[:, b, a, :], ACT.Exp, bias=stat[:, b, 2 + a:3 + a],
                                       accum_out=stat[:, b, 4 + a:5 + a])
                e.then_inc(exp_ready.sem, 1)

            def weights_out(here, h):
                act.wait_ge(p_turned.sem, here.at(p_turned, h + 1))
                if h >= 2:
                    act.wait_ge(pv_done.sem, here.at(pv_done, h - 1))
                act.activation(softT[:, h % 2, :, :], banks[6][:, :, :], ACT.Copy).then_inc(pT_ready.sem, 1)

            def attention_out(here, j):
                act.wait_ge(pv_done.sem, here.at(pv_done, 2 * j + 2))
                act.activation(att_hi[:, j, :], banks[7][:, j % 2, :], ACT.Copy).then_inc(att_hi_ready.sem, 1)

            def merged_upper(here, merged, j):
                act.wait_ge(merged_ready.sem, here.at(merged_ready, j + 1))
                act.activation(in_hi[:, 2 * j:2 * j + 2, :], merged[:, 2 * j:2 * j + 2, :], ACT.Copy
                               ).then_inc(merged_hi.sem, 1)

            act.wait_ge(small_set, 3 + len(WINDOWS))
            act.wait_ge(x_in, 16)
            for j in range(HALVES):
                act.activation(work[:, 2 * j:2 * j + 2, :], x[:, 2 * j:2 * j + 2, :], ACT.Square
                               ).then_inc(sq_ready.sem, 1)
            for s in range(2):
                split_hi(s, 0)

            with act.Fori(0, DEPTH) as layer:
                here = Place(0, layer)
                norm(here, 0)
                split_hi(2, here.uses(2))
                ffn(here, 0, 0)
                squares(here, 0, range(HALVES))
                norm(here, 1)
                split_hi(2, here.uses(FFN_CHUNKS + 2))
                for m in range(MIX1):
                    c = FFN_CHUNKS + m
                    chunk_done(here, c)
                    bank = banks[4 + m % 2]
                    if m < 4:
                        act.activation(qk[:, 2 * m:2 * m + 2, :], bank[:, :, :], ACT.Copy).then_inc(mix_evac.sem, 1)
                        if m >= 2:
                            act.wait_ge(qk_ms.sem, here.at(qk_ms, m - 1))
                        act.activation(qk_sq[:, m % 2, :], flat(bank[:, :, :]), ACT.Square).then_inc(qk_sq_ready.sem, 1)
                    elif m < 6:
                        act.activation(v_tok[:, :, (m - 4) * T:(m - 3) * T], bank[:, :, :], ACT.Copy
                                       ).then_inc(mix_evac.sem, 1)
                    elif m < 8:
                        act.activation(u[:, 2 * (m - 6):2 * (m - 5), :], bank[:, :, :], ACT.Copy).then_inc(mix_evac.sem, 1)
                    elif m < 12 or 14 <= m < 18:
                        branch, j = (0, m - 8) if m < 12 else (1, m - 14)
                        if m == 14:
                            act.wait_ge(branch_evac.sem, here.at(branch_evac, 2))
                        for a in range(2):
                            f = 2 * j + a
                            col = C_GATE + DT * branch + f
                            e = act.activation(gates1[:, f, :], bank[:, a, :], ACT.Identity, bias=cur[:, col:col + 1])
                        e.then_inc(mix_evac.sem, 1)
                    if 1 <= m < 5:
                        act.wait_ge(qk_ms.sem, here.at(qk_ms, m))
                        if m >= 2:
                            act.wait_ge(qk_rstd.sem, here.at(qk_rstd, m - 1))
                        act.activation(tmp[:, :], flat(banks[0][:, :, :]), ACT.Sqrt, bias=eps6).then_inc(qk_sd.sem, 1)
                    if m == 10:
                        act.wait_ge(pool_y.sem, here.at(pool_y, 1))
                        for g in range(4):
                            act.activation(br_hi[:, g, :], banks[g // 2][:, g % 2, :], ACT.Copy,
                                           scale=cur[:, C_SCALE + g:C_SCALE + g + 1]).then_inc(pool_hi.sem, 1)
                    if 0 <= m - 8 < HEADS:
                        weights_out(here, m - 8)
                    if m >= 10 and m % 2 == 0 and (m - 10) // 2 < HALVES:
                        attention_out(here, (m - 10) // 2)
                    if 0 <= m - 7 < HEADS:
                        softmax_exp(here, m - 7)
                    if m in (11, 17):
                        act.wait_ge(mix_evac.sem, here.at(mix_evac, 12 if m == 11 else 16))
                        act.activation(gates1[:, :, :], gates1[:, :, :], ACT.Sigmoid).then_inc(sig_ready.sem, 1)
                    if m in (18, 19):
                        for j in range(2 * (m - 18), 2 * (m - 17)):
                            merged_upper(here, merged1, j)
                    if m >= 20:
                        squares(here, 1, [m - 20])
                    if m < MIX1 - 1:
                        split_after(here, c)
                norm(here, 2)
                split_hi(2, here.uses(FFN_CHUNKS + MIX1 + 2))
                ffn(here, FFN_CHUNKS + MIX1, 1)
                squares(here, 2, range(HALVES))

            for k in range(DT):
                act.activation(in_hi[:, k, :], x[:, k, :], ACT.Copy).then_inc(xs_hi.sem, 1)
            act.wait_ge(col_in, 32)
            last = col2[:, :, C_LF:COLS2]
            steps = [decay[:, n, :].rearrange("p (l c) -> p l c", l=DEPTH) for n in range(4)]
            act.activation(steps[0], last, ACT.Abs).then_inc(decay_scal, 1)
            act.wait_ge(decay_scal, 1)
            act.activation(steps[1], steps[0], ACT.Exp, scale=-1.0).then_inc(decay_scal, 1)
            act.wait_ge(decay_scal, 2)
            act.activation(steps[2], steps[1], ACT.Ln, bias=1.0).then_inc(decay_scal, 1)

            with act.Fori(0, DEPTH) as layer:
                here = Place(1, layer)
                act.wait_ge(xs_ready.sem, here.at(xs_ready, 0))
                split_hi(2, here.uses(2))

                def layer_norm(n, col_b, spare=lambda: None):
                    act.wait_ge(var_ready.sem, here.at(var_ready, n + 1))
                    act.activation(spread[:, :], banks[7][:, 0, :], ACT.Sqrt, bias=eps5).then_inc(ln_sd.sem, 1)
                    spare()
                    for k in range(DT):
                        act.wait_ge(ln_scaled.sem, here.at(ln_scaled, DT * n + k + 1))
                        act.activation(x[:, k, :], work[:, k, :], ACT.Identity, bias=cur[:, col_b + k:col_b + k + 1]
                                       ).then_inc(x_new.sem, 1)
                        act.activation(in_hi[:, k, :], work[:, k, :], ACT.Identity,
                                       bias=cur[:, col_b + k:col_b + k + 1]).then_inc(xs_hi.sem, 1)

                def centred_squares(n):
                    for k in range(DT):
                        act.wait_ge(c_ready.sem, here.at(c_ready, DT * n + k + 1))
                        act.activation(work[:, k, :], x[:, k, :], ACT.Square).then_inc(c_sq.sem, 1)

                for m in range(MIX2):
                    chunk_done(here, m)
                    bank = banks[4 + m % 2]
                    if m < 4:
                        act.activation(qk[:, 2 * m:2 * m + 2, :], bank[:, :, :], ACT.Copy).then_inc(mix_evac.sem, 1)
                    elif m < 6:
                        act.activation(v_tok[:, :, (m - 4) * T:(m - 3) * T], bank[:, :, :], ACT.Copy
                                       ).then_inc(mix_evac.sem, 1)
                    elif m < 10:
                        act.activation(ret_qk[:, 2 * (m - 6):2 * (m - 5), :], bank[:, :, :], ACT.Copy
                                       ).then_inc(mix_evac.sem, 1)
                    elif m < 14:
                        if m == 13:
                            act.wait_ge(qk_ready.sem, here.at(qk_ready, 4))
                        act.activation(ret_v[:, :, (m - 10) * T:(m - 9) * T], bank[:, :, :], ACT.Copy
                                       ).then_inc(mix_evac.sem, 1)
                    elif m < 18:
                        if m == 14:
                            act.wait_ge(masked.sem, here.at(masked, HEADS))
                        act.activation(silu_g[:, 2 * (m - 14):2 * (m - 13), :], bank[:, :, :], ACT.Silu
                                       ).then_inc(mix_evac.sem, 1)
                    elif m < 22 or 24 <= m < 28:
                        j = m - 18 if m < 22 else m - 24
                        if m == 24:
                            act.wait_ge(branch_evac.sem, here.at(branch_evac, 2))
                        act.activation(gates2[:, 2 * j:2 * j + 2, :], bank[:, :, :], ACT.Sigmoid).then_inc(mix_evac.sem, 1)
                    elif m == 28:
                        act.wait_ge(ple_in_sem, (layer + 1) * 16)
                        act.activation(ple_hi[:, :, :], ple_in[:, :, :], ACT.Copy).then_inc(ple_split_hi.sem, 1)
                    elif m >= 38:
                        j = m - 38
                        if m >= 40:
                            act.wait_ge(ple_mul.sem, here.at(ple_mul, j - 1))
                        act.activation(ple_gate[:, j % 2, :], flat(bank[:, :, :]), ACT.Sigmoid).then_inc(mix_evac.sem, 1)
                    if 4 <= m < 4 + RET_HEADS:
                        h = m - 4
                        act.wait_ge(dist_ready.sem, here.at(dist_ready, h + 1))
                        act.activation(decays[:, h, :], decays[:, h, :], ACT.Exp).then_inc(decay_ready.sem, 1)
                    if 0 <= m - 6 < HEADS:
                        weights_out(here, m - 6)
                    if m >= 8 and m % 2 == 0 and (m - 8) // 2 < HALVES:
                        attention_out(here, (m - 8) // 2)
                    if 0 <= m - 5 < HEADS:
                        softmax_exp(here, m - 5)
                    if 0 <= m - 18 < RET_HEADS:
                        h = m - 18
                        act.wait_ge(ret_y.sem, here.at(ret_y, h + 1))
                        act.activation(br_hi[:, 2 * h:2 * h + 2, :], soft[:, h % 2, :, :], ACT.Copy).then_inc(ret_hi.sem, 1)
                    if 28 <= m < 32:
                        merged_upper(here, merged2, m - 28)
                    if m == 35:
                        split_after(here, m)
                        centred_squares(0)
                    elif m == 36:
                        def ple_first():
                            for a in range(2):
                                e = act.activation(ple_out[:, 2 * a:2 * a + 2, :], banks[4 + a][:, :, :], ACT.Copy)
                            e.then_inc(mix_evac.sem, 1)
                        layer_norm(0, C_B1, ple_first)
                        split_after(here, m)
                    elif m == 37:
                        for a in range(2):
                            e = act.activation(ple_out[:, 4 + 2 * a:6 + 2 * a, :], banks[2 + a][:, :, :], ACT.Copy)
                        e.then_inc(mix_evac.sem, 1)
                        split_after(here, m)
                    else:
                        split_after(here, m)

                def step(kind, i, c, turn):
                    final = c == CHUNKS[1] - 1
                    if not final:
                        chunk_done(here, c, turn)
                    if kind == "A":
                        for a in range(2):
                            mid = cur[:, bass.ds(i * 2 + (C_TAP + FT + a), 1)]
                            add = cur[:, bass.ds(i * 2 + (C_CONVB + a), 1)]
                            e = act.activation(glu_a[:, a, :], banks[4][:, a, :], ACT.Identity, bias=add, scale=mid)
                        e.then_inc(gate_act.sem, 1)
                    if kind == "B":
                        for a in range(2):
                            mid = cur[:, bass.ds(i * 2 + (C_TAP + FT + FT // 2 + a), 1)]
                            add = cur[:, bass.ds(i * 2 + (C_CONVB + FT // 2 + a), 1)]
                            e = act.activation(glu_b[:, a, :], banks[5][:, a, :], ACT.Identity, bias=add, scale=mid)
                        e.then_inc(up_mid.sem, 1)
                        act.wait_ge(gate_taps.sem, here.at(gate_taps, i + 1))
                        act.activation(glu_a, glu_a, ACT.Gelu_apprx_tanh).then_inc(gelu_ready.sem, 1)
                        if c == MIX2 + 1:
                            hidden_upper(here, 0)
                    if kind == "D" and not final:
                        hidden_upper(here, i + 1)
                    if c in (CHUNKS[1] - 3, CHUNKS[1] - 2):
                        with act.If(layer < DEPTH - 1):
                            split_after(here, c, turn)
                    elif not final:
                        split_after(here, c, turn)
                ffn_walk(act, MIX2, step)
                centred_squares(1)
                layer_norm(1, C_B2)

        @block.vector
        def _(dve):
            def split_lo(s, uses):
                dve.wait_ge(hi_ready[s], uses + 1)
                dve.tensor_tensor(w_lo[:, s, :], raw[:, s, :], w_hi[:, s, :].bitcast(F32), ALU.subtract
                                  ).then_inc(lo_ready[s], 1)

            def chunk_done(here, c, turn=0):
                dve.wait_ge(w_used[c % SLOTS], here.uses(c, turn) + 1)

            def split_after(here, c, turn=0):
                split_lo(c % SLOTS, here.uses(c, turn) + 1)

            def rest(out, whole, upper):
                return dve.tensor_tensor(out, whole, upper.bitcast(F32), ALU.subtract)

            def norm(here, n, col):
                dve.wait_ge(sd_ready.sem, here.at(sd_ready, n + 1))
                dve.reciprocal(rstd[:, :], spread[:, :]).then_inc(rstd_ready.sem, 1)
                dve.wait_ge(rstd_ready.sem, here.at(rstd_ready, n + 1))

                def lower(k):
                    dve.wait_ge(xn_hi.sem, here.at(xn_hi, DT * n + k + 1))
                    rest(in_lo[:, k, :], work[:, k, :], in_hi[:, k, :]).then_inc(xn_ready.sem, 1)

                for k in range(DT):
                    dve.scalar_tensor_tensor(out=work[:, k, :], in0=x[:, k, :], scalar=cur[:, col + k:col + k + 1],
                                             in1=rstd[:, :], op0=ALU.mult, op1=ALU.mult).then_inc(xnf_ready.sem, 1)
                    if k >= 1:
                        lower(k - 1)
                lower(DT - 1)

            def hidden_lower(here, n):
                dve.wait_ge(hid_hi_ready.sem, here.at(hid_hi_ready, n + 1))
                rest(hid_lo[:, :, :], hidden, hid_hi[:, :, :]).then_inc(hid_ready.sem, 1)

            def ffn(here, c0, f, stage):
                def step(kind, i, c, turn):
                    final = c == c0 + FFN_CHUNKS - 1
                    if not final:
                        chunk_done(here, c, turn)
                    if kind == "B":
                        dve.wait_ge(gate_act.sem, here.at(gate_act, i + (f * PAIRS + 1)))
                        if c != c0 + 1:
                            dve.wait_ge(hid_ready.sem, here.at(hid_ready, i + f * PAIRS))
                        dve.tensor_tensor(hidden, glu_a, banks[5][:, :, :], ALU.mult).then_inc(prod_ready.sem, 1)
                        if c == c0 + 1:
                            hidden_lower(here, f * PAIRS)
                    if kind == "D" and not final:
                        hidden_lower(here, i + (f * PAIRS + 1))
                    if not final:
                        split_after(here, c, turn)
                    else:
                        for j in range(HALVES):
                            if j < HALVES - 1:
                                dve.wait_ge(acc_done.sem, here.at(acc_done, f * (HALVES - 1) + j + 1))
                            else:
                                chunk_done(here, c)
                            two = x[:, 2 * j:2 * j + 2, :]
                            dve.scalar_tensor_tensor(out=two, in0=banks[j][:, :, :], scalar=0.5, in1=two, op0=ALU.mult,
                                                     op1=ALU.add).then_inc(x_ready.sem, 1)
                ffn_walk(dve, c0, step)

            def softmax_scores(here, h, score_bias):
                b = h % 2
                dve.wait_ge(scored.sem, here.at(scored, h + 1))
                if h >= 2:
                    dve.wait_ge(p_turned.sem, here.at(p_turned, h - 1))
                score_bias(b)
                dve.wait_ge(masked.sem, here.at(masked, h + 1))
                dve.tensor_reduce(stat[:, b, 0:2], soft[:, b, :, :], axis=AX_X, op=ALU.max).then_inc(max_ready.sem, 1)
                dve.wait_ge(max_ready.sem, here.at(max_ready, h + 1))
                dve.tensor_scalar(stat[:, b, 2:4], stat[:, b, 0:2], -1.0, None, ALU.mult).then_inc(nmax_ready.sem, 1)

            def softmax_weights(here, h):
                b = h % 2
                dve.wait_ge(exp_ready.sem, here.at(exp_ready, h + 1))
                dve.reciprocal(stat[:, b, 6:8], stat[:, b, 4:6]).then_inc(inv_ready.sem, 1)
                dve.wait_ge(inv_ready.sem, here.at(inv_ready, h + 1))
                dve.tensor_tensor(soft[:, b, :, :], soft[:, b, :, :],
                                  stat[:, b, 6:8].unsqueeze(2).broadcast_to([P, TT, T]), ALU.mult).then_inc(p_ready.sem, 1)

            def attention_lower(here, j):
                dve.wait_ge(att_hi_ready.sem, here.at(att_hi_ready, j + 1))
                rest(att_lo[:, j, :], banks[7][:, j % 2, :], att_hi[:, j, :]).then_inc(att_ready.sem, 1)

            def turn_pairs(here, n, two, turned, cos, sin, bank):
                dve.wait_ge(qk_rot.sem, here.at(qk_rot, n + 1))
                dve.tensor_tensor(turned[:, :, :], bank[:, :, :], table(sin), ALU.mult).then_inc(qk_sin.sem, 1)
                dve.tensor_tensor(two, two, table(cos), ALU.mult).then_inc(qk_cos.sem, 1)
                dve.wait_ge(qk_sin.sem, here.at(qk_sin, n + 1))
                dve.wait_ge(qk_cos.sem, here.at(qk_cos, n + 1))
                dve.tensor_tensor(two, two, turned[:, :, :], ALU.add).then_inc(qk_ready.sem, 1)

            def merged_lower(here, merged, j):
                dve.wait_ge(merged_hi.sem, here.at(merged_hi, j + 1))
                rest(in_lo[:, 2 * j:2 * j + 2, :], merged[:, 2 * j:2 * j + 2, :], in_hi[:, 2 * j:2 * j + 2, :]
                     ).then_inc(merged_lo.sem, 1)

            dve.wait_ge(col_in, 32)
            dve.wait_ge(konst_in, 16)
            dve.wait_ge(x_in, 16)
            for s in range(2):
                split_lo(s, 0)

            with dve.Fori(0, DEPTH) as layer:
                here = Place(0, layer)
                dve.tensor_copy(cur[:, 0:COLS1], col1[:, bass.ds(layer, 1), :].rearrange("p a c -> p (a c)")
                                ).then_inc(cur_ready.sem, 1)
                dve.wait_ge(cur_ready.sem, here.at(cur_ready, 1))
                norm(here, 0, C_FFN1)
                split_lo(2, here.uses(2))
                ffn(here, 0, 0, 0)
                dve.wait_ge(x_ready.sem, here.at(x_ready, HALVES))
                norm(here, 1, C_MIX)
                split_lo(2, here.uses(FFN_CHUNKS + 2))
                for m in range(MIX1):
                    c = FFN_CHUNKS + m
                    chunk_done(here, c)
                    if 0 <= m - 7 < HEADS:
                        def causal_scores(b, h=m - 7):
                            dve.scalar_tensor_tensor(out=soft[:, b, :, :], in0=banks[2 + b][:, :, :], scalar=HEAD_DIM ** -0.5,
                                                     in1=causal, op0=ALU.mult, op1=ALU.add).then_inc(masked.sem, 1)
                        softmax_scores(here, m - 7, causal_scores)
                    if 2 <= m < 6:
                        turn_pairs(here, m - 2, qk[:, 2 * (m - 2):2 * (m - 1), :], softT[:, 0, :, :], K_COS1, K_SIN1,
                                   banks[1])
                    if 1 <= m < 5:
                        p = m - 1
                        dve.wait_ge(qk_sd.sem, here.at(qk_sd, p + 1))
                        inv = softT[:, 1, :, :]
                        dve.reciprocal(flat(inv), tmp[:, :]).then_inc(qk_rstd.sem, 1)
                        dve.wait_ge(qk_rstd.sem, here.at(qk_rstd, p + 1))
                        col = C_Q if p < 2 else C_K
                        two = qk[:, 2 * p:2 * p + 2, :]
                        dve.scalar_tensor_tensor(out=two, in0=two, scalar=cur[:, col:col + 1], in1=inv, op0=ALU.mult,
                                                 op1=ALU.mult).then_inc(qk_normed.sem, 1)
                    if m == 10:
                        dve.wait_ge(pool_hi.sem, here.at(pool_hi, 4))
                        for g in range(4):
                            e = dve.scalar_tensor_tensor(out=br_lo[:, g, :], in0=banks[g // 2][:, g % 2, :],
                                                         scalar=cur[:, C_SCALE + g:C_SCALE + g + 1],
                                                         in1=br_hi[:, g, :].bitcast(F32), op0=ALU.mult, op1=ALU.subtract)
                        e.then_inc(pool_ready.sem, 1)
                    if m in (12, 13):
                        if m == 12:
                            dve.wait_ge(sig_ready.sem, here.at(sig_ready, 1))
                        for a in range(2):
                            f = 4 * (m - 12) + 2 * a
                            e = dve.tensor_tensor(merged1[:, f:f + 2, :], gates1[:, f:f + 2, :],
                                                  banks[4 * (m - 12) + a][:, :, :], ALU.mult)
                        e.then_inc(branch_evac.sem, 1)
                    if m in (18, 19):
                        if m == 18:
                            dve.wait_ge(sig_ready.sem, here.at(sig_ready, 2))
                            dve.wait_ge(branch_evac.sem, here.at(branch_evac, 2))
                        for a in range(2):
                            j = 2 * (m - 18) + a
                            f = 2 * j
                            part = gates1[:, f:f + 2, :]
                            e = dve.tensor_tensor(part, part, banks[4 * (m - 18) + a][:, :, :], ALU.mult
                                                  ).then_inc(part_ready.sem, 1)
                            dve.wait_ge(part_ready.sem, here.at(part_ready, j + 1))
                            dve.tensor_tensor(merged1[:, f:f + 2, :], merged1[:, f:f + 2, :], part, ALU.add
                                              ).then_inc(merged_ready.sem, 1)
                        for a in range(2):
                            merged_lower(here, merged1, 2 * (m - 18) + a)
                        dve.sem_inc(branch_evac.sem, 1)
                    if m >= 10 and m % 2 == 0 and (m - 10) // 2 < HALVES:
                        attention_lower(here, (m - 10) // 2)
                    if 0 <= m - 7 < HEADS:
                        softmax_weights(here, m - 7)
                    if m >= 20:
                        two = x[:, 2 * (m - 20):2 * (m - 19), :]
                        dve.tensor_tensor(two, two, banks[m - 20][:, :, :], ALU.add).then_inc(x_ready.sem, 1)
                    if m < MIX1 - 1:
                        split_after(here, c)
                dve.wait_ge(x_ready.sem, here.at(x_ready, 2 * HALVES))
                norm(here, 2, C_FFN2)
                split_lo(2, here.uses(FFN_CHUNKS + MIX1 + 2))
                ffn(here, FFN_CHUNKS + MIX1, 1, 2)
                dve.wait_ge(x_ready.sem, here.at(x_ready, 3 * HALVES))

            for k in range(DT):
                dve.wait_ge(xs_hi.sem, DEPTH * 0 + k + 1)
                rest(in_lo[:, k, :], x[:, k, :], in_hi[:, k, :]).then_inc(xs_ready.sem, 1)
            steps = [decay[:, n, :].rearrange("p (l c) -> p l c", l=DEPTH) for n in range(4)]
            last = col2[:, :, C_LF:COLS2]
            dve.wait_ge(decay_scal, 3)
            dve.tensor_scalar(steps[3], last, 0.0, None, ALU.min).then_inc(decay_step, 1)
            dve.wait_ge(decay_step, 1)
            dve.tensor_tensor(last[:, :, 0:RET_HEADS], steps[3][:, :, 0:RET_HEADS], steps[2][:, :, 0:RET_HEADS],
                              ALU.subtract).then_inc(decay_step, 1)
            dve.tensor_tensor(last[:, :, RET_HEADS:], steps[2][:, :, RET_HEADS:], steps[3][:, :, RET_HEADS:],
                              ALU.subtract).then_inc(decay_step, 1)
            dve.wait_ge(decay_step, 3)

            with dve.Fori(0, DEPTH) as layer:
                here = Place(1, layer)
                dve.tensor_copy(cur[:, 0:COLS2], col2[:, bass.ds(layer, 1), :].rearrange("p a c -> p (a c)")
                                ).then_inc(cur_ready.sem, 1)
                dve.wait_ge(cur_ready.sem, here.at(cur_ready, 1))
                split_lo(2, here.uses(2))

                def centred(n):
                    dve.wait_ge(mu_ready.sem, here.at(mu_ready, n + 1))
                    for k in range(DT):
                        dve.tensor_tensor(x[:, k, :], x[:, k, :], banks[6][:, 0, :], ALU.subtract).then_inc(c_ready.sem, 1)

                def layer_norm(n, col):
                    dve.wait_ge(ln_sd.sem, here.at(ln_sd, n + 1))
                    dve.reciprocal(rstd[:, :], spread[:, :]).then_inc(ln_rstd.sem, 1)
                    dve.wait_ge(ln_rstd.sem, here.at(ln_rstd, n + 1))

                    def lower(k):
                        dve.wait_ge(xs_hi.sem, here.at(xs_hi, DT * n + k + 1))
                        rest(in_lo[:, k, :], x[:, k, :], in_hi[:, k, :]).then_inc(xs_ready.sem, 1)

                    for k in range(DT):
                        dve.scalar_tensor_tensor(out=work[:, k, :], in0=x[:, k, :], scalar=cur[:, col + k:col + k + 1],
                                                 in1=rstd[:, :], op0=ALU.mult, op1=ALU.mult).then_inc(ln_scaled.sem, 1)
                        if k >= 1:
                            lower(k - 1)
                    lower(DT - 1)

                for m in range(MIX2):
                    chunk_done(here, m)
                    if 0 <= m - 5 < HEADS:
                        def near_scores(b, h=m - 5):
                            if h == 0:
                                dve.wait_ge(bias_ready.sem, here.at(bias_ready, 1))
                            for a in range(TT):
                                r = (TT - 1 - a) * (P // GRID_W)
                                e = dve.scalar_tensor_tensor(
                                    out=soft[:, b, a, :].rearrange("p (r c) -> p r c", c=GRID_W),
                                    in0=banks[2 + b][:, a, :].rearrange("p (r c) -> p r c", c=GRID_W),
                                    scalar=HEAD_DIM ** -0.5, in1=bias[:, h, r:r + GRID_ROWS, :], op0=ALU.mult, op1=ALU.add)
                            e.then_inc(masked.sem, 1)
                        softmax_scores(here, m - 5, near_scores)
                    if 7 <= m < 11:
                        if m == 7:
                            dve.wait_ge(dist_ready.sem, here.at(dist_ready, RET_HEADS))
                        turn_pairs(here, m - 7, ret_qk[:, 2 * (m - 7):2 * (m - 6), :], ret_turn, K_COS2, K_SIN2,
                                   banks[(m - 7) % 2])
                    if 0 <= m - 15 < RET_HEADS:
                        h = m - 15
                        dve.wait_ge(ret_scored.sem, here.at(ret_scored, h + 1))
                        dve.wait_ge(decay_ready.sem, here.at(decay_ready, h + 1))
                        if h >= 2:
                            dve.wait_ge(ret_pv.sem, here.at(ret_pv, h - 1))
                        dve.scalar_tensor_tensor(out=flat(softT[:, h % 2, :, :]), in0=flat(banks[2 + h % 2][:, :, :]),
                                                 scalar=RET_QK ** -0.5, in1=decays[:, h, :], op0=ALU.mult, op1=ALU.mult
                                                 ).then_inc(ret_p.sem, 1)
                    if 0 <= m - 18 < RET_HEADS:
                        h = m - 18
                        dve.wait_ge(ret_turned.sem, here.at(ret_turned, h + 1))
                        dve.tensor_tensor(soft[:, h % 2, :, :], banks[6][:, :, :], silu_g[:, 2 * h:2 * h + 2, :], ALU.mult
                                          ).then_inc(ret_y.sem, 1)
                        dve.wait_ge(ret_hi.sem, here.at(ret_hi, h + 1))
                        rest(br_lo[:, 2 * h:2 * h + 2, :], soft[:, h % 2, :, :], br_hi[:, 2 * h:2 * h + 2, :]
                             ).then_inc(ret_ready.sem, 1)
                    if 0 <= m - 16 < RET_HEADS:
                        h = m - 16
                        b = h % 2
                        dve.wait_ge(ret_pv.sem, here.at(ret_pv, h + 1))
                        for a in range(TT):
                            e = dve.bn_stats(group[:, b, a, 0:6], banks[b][:, a, :])
                        e.then_inc(ret_stats.sem, 1)
                        dve.wait_ge(ret_stats.sem, here.at(ret_stats, h + 1))
                        dve.memset(group[:, b, :, 8:9], GN_EPS)
                        for a in range(TT):
                            e = dve.bn_aggr(group[:, b, a, 6:8], group[:, b, a, 0:6])
                        e.then_inc(ret_mv.sem, 1)
                        dve.wait_ge(ret_mv.sem, here.at(ret_mv, h + 1))
                        dve.tensor_tensor(group[:, b, :, 10:11], group[:, b, :, 7:8], group[:, b, :, 8:9], ALU.add
                                          ).then_inc(ret_var.sem, 1)
                        dve.wait_ge(ret_rstd.sem, here.at(ret_rstd, h + 1))
                        for a in range(TT):
                            e = dve.tensor_scalar(soft[:, b, a, :], banks[b][:, a, :], group[:, b, a, 6:7],
                                                  group[:, b, a, 11:12], ALU.subtract, ALU.mult)
                        e.then_inc(ret_o.sem, 1)
                    if m in (22, 23):
                        for a in range(2):
                            f = 4 * (m - 22) + 2 * a
                            if a == 0:
                                dve.wait_ge(mix_evac.sem, here.at(mix_evac, 22))
                            e = dve.tensor_tensor(merged2[:, f:f + 2, :], gates2[:, f:f + 2, :],
                                                  banks[4 * (m - 22) + a][:, :, :], ALU.mult)
                        e.then_inc(branch_evac.sem, 1)
                    if m == 28:
                        dve.wait_ge(ple_split_hi.sem, here.at(ple_split_hi, 1))
                        rest(ple_lo[:, :, :], ple_in[:, :, :], ple_hi[:, :, :]).then_inc(ple_split.sem, 1)
                    if 28 <= m < 32:
                        j = m - 28
                        f = 2 * j
                        part = gates2[:, f:f + 2, :]
                        dve.wait_ge(mix_evac.sem, here.at(mix_evac, 26))
                        dve.tensor_tensor(part, part, banks[j % 2][:, :, :], ALU.mult).then_inc(branch_evac.sem, 1)
                        dve.wait_ge(branch_evac.sem, here.at(branch_evac, 3 + j))
                        dve.tensor_tensor(merged2[:, f:f + 2, :], merged2[:, f:f + 2, :], part, ALU.add
                                          ).then_inc(merged_ready.sem, 1)
                        merged_lower(here, merged2, j)
                    if 32 <= m < 36:
                        two = x[:, 2 * (m - 32):2 * (m - 31), :]
                        dve.scalar_tensor_tensor(out=two, in0=two, scalar=ALPHA, in1=banks[m - 32][:, :, :], op0=ALU.mult,
                                                 op1=ALU.add).then_inc(z_ready.sem, 1)
                    if m >= 38:
                        j = m - 38
                        two = ple_out[:, 2 * j:2 * j + 2, :]
                        dve.wait_ge(mix_evac.sem, here.at(mix_evac, 29 + j))
                        dve.tensor_tensor(flat(two), flat(two), ple_gate[:, j % 2, :], ALU.mult).then_inc(ple_mul.sem, 1)
                        dve.wait_ge(ple_mul.sem, here.at(ple_mul, j + 1))
                        dve.scalar_tensor_tensor(out=x[:, 2 * j:2 * j + 2, :], in0=x[:, 2 * j:2 * j + 2, :], scalar=ALPHA,
                                                 in1=two, op0=ALU.mult, op1=ALU.add).then_inc(base_ready.sem, 1)
                    if m >= 8 and m % 2 == 0 and (m - 8) // 2 < HALVES:
                        attention_lower(here, (m - 8) // 2)
                    if 0 <= m - 5 < HEADS:
                        softmax_weights(here, m - 5)
                    if m == 35:
                        centred(0)
                        split_after(here, m)
                    elif m == 36:
                        layer_norm(0, C_G1)
                        split_after(here, m)
                    else:
                        split_after(here, m)

                def taps(out, bank, i, first, left, done, n):
                    for a in range(2):
                        w = cur[:, bass.ds(i * 2 + (first + a), 1)]
                        e = dve.scalar_tensor_tensor(out=out[:, a, 1:T], in0=bank[:, a, 0:T - 1], scalar=w,
                                                     in1=out[:, a, 1:T], op0=ALU.mult, op1=ALU.add)
                    e.then_inc(left.sem, 1)
                    dve.wait_ge(left.sem, here.at(left, n))
                    for a in range(2):
                        w = cur[:, bass.ds(i * 2 + (first + 2 * FT + a), 1)]
                        e = dve.scalar_tensor_tensor(out=out[:, a, 0:T - 1], in0=bank[:, a, 1:T], scalar=w,
                                                     in1=out[:, a, 0:T - 1], op0=ALU.mult, op1=ALU.add)
                    e.then_inc(done.sem, 1)

                def step(kind, i, c, turn):
                    final = c == CHUNKS[1] - 1
                    if not final:
                        chunk_done(here, c, turn)
                    if kind == "A":
                        dve.wait_ge(gate_act.sem, here.at(gate_act, i + 1))
                        taps(glu_a, banks[4], i, C_TAP, gate_left, gate_taps, i + 1)
                    if kind == "B":
                        dve.wait_ge(up_mid.sem, here.at(up_mid, i + 1))
                        taps(glu_b, banks[5], i, C_TAP + FT // 2, up_left, up_taps, i + 1)
                        dve.wait_ge(up_taps.sem, here.at(up_taps, i + 1))
                        dve.wait_ge(gelu_ready.sem, here.at(gelu_ready, i + 1))
                        if c != MIX2 + 1:
                            dve.wait_ge(hid_ready.sem, here.at(hid_ready, i))
                        dve.tensor_tensor(hidden, glu_a, glu_b, ALU.mult).then_inc(prod_ready.sem, 1)
                        if c == MIX2 + 1:
                            hidden_lower(here, 0)
                    if kind == "D" and not final:
                        hidden_lower(here, i + 1)
                    if c in (CHUNKS[1] - 3, CHUNKS[1] - 2):
                        with dve.If(layer < DEPTH - 1):
                            split_after(here, c, turn)
                    elif not final:
                        split_after(here, c, turn)
                    else:
                        dve.wait_ge(base_ready.sem, here.at(base_ready, 4))
                        for j in range(HALVES):
                            if j < HALVES - 1:
                                dve.wait_ge(acc_done.sem, here.at(acc_done, j + 1))
                            else:
                                chunk_done(here, c)
                            two = x[:, 2 * j:2 * j + 2, :]
                            dve.tensor_tensor(two, two, banks[j][:, :, :], ALU.add).then_inc(z_ready.sem, 1)
                ffn_walk(dve, MIX2, step)
                centred(1)
                layer_norm(1, C_G2)

        @block.tensor
        def _(pe):
            def take(here, c, turn=0):
                pe.wait_ge(lo_ready[c % SLOTS], here.uses(c, turn) + 1)

            def product(out, whi, wlo, xhi, xlo, start, stop):
                pe.matmul(out, whi, xlo, start=start, stop=False, skip_group_check=True)
                pe.matmul(out, wlo, xhi, start=False, stop=False, skip_group_check=True)
                return pe.matmul(out, whi, xhi, start=False, stop=stop, skip_group_check=True)

            def features(c, outs, hi, lo, tiles, k_first=None, fresh=True, stop=True, tile_done=None):
                s, width = c % SLOTS, len(outs) * P

                def one(f, k):
                    at = k * width + f * P
                    return product(outs[f], w_hi[:, s, at:at + P], w_lo[:, s, at:at + P], hi[:, k, :], lo[:, k, :],
                                   start=fresh and k == 0 and f % 2 == 0, stop=stop and k == tiles - 1)

                if k_first is not None:
                    for k in range(tiles):
                        k_first(k)
                        for f in range(len(outs)):
                            e = one(f, k)
                else:
                    for f in range(len(outs)):
                        for k in range(tiles):
                            e = one(f, k)
                        if tile_done and f < len(outs) - 1:
                            tile_done(f, e)
                return e.then_inc(w_used[s], 1)

            def two(bank):
                return [bank[:, a, :] for a in range(2)]

            acc = [banks[f // 2][:, f % 2, :] for f in range(DT)]

            def tokens(c, bank, hi, lo):
                s = c % SLOTS
                for a in range(TT):
                    for k in range(DT):
                        rows, cols = slice(a * P, (a + 1) * P), slice(k * T, (k + 1) * T)
                        e = product(bank[:, a, :], hi[:, k, rows], lo[:, k, rows], w_hi[:, s, cols], w_lo[:, s, cols],
                                    start=a == 0 and k == 0, stop=k == DT - 1)
                return e.then_inc(w_used[s], 1)

            def square_mean(here, stage, j):
                pe.wait_ge(sq_ready.sem, here.at(sq_ready, HALVES * stage + j + 1) if here else j + 1)
                for f in (2 * j, 2 * j + 1):
                    e = pe.matmul(banks[6][:, 0, :], mean_of, work[:, f, :], start=f == 0, stop=f == DT - 1)
                if j == HALVES - 1:
                    e.then_inc(ss_ready.sem, 1)

            def ffn_final(here, c, f, between):
                s = c % SLOTS
                for t in range(DT):
                    for k in range(2):
                        at = k * D + t * P
                        e = product(acc[t], w_hi[:, s, at:at + P], w_lo[:, s, at:at + P], hid_hi[:, k, :],
                                    hid_lo[:, k, :], start=False, stop=k == 1)
                    if t % 2:
                        e.then_inc(acc_done.sem if t < DT - 1 else w_used[s], 1)
                        if t >= 3:
                            between(t // 2 - 1)
                between(HALVES - 1)

            def ffn(here, c0, f, first, read_gate, read_up, between):
                def step(kind, i, c, turn):
                    take(here, c, turn)
                    if kind == "D":
                        pe.wait_ge(hid_ready.sem, here.at(hid_ready, i + (f * PAIRS + 1)))
                        if c == c0 + FFN_CHUNKS - 1:
                            ffn_final(here, c, f, between)
                        else:
                            features(c, acc, hid_hi, hid_lo, 2, fresh=c == c0 + 4, stop=False)
                    elif c == c0:
                        features(c, two(banks[4]), in_hi, in_lo, DT, k_first=first)
                    else:
                        if kind == "A":
                            pe.wait_ge(read_gate.sem, here.at(read_gate, i + f * PAIRS))
                        elif c != c0 + 1:
                            pe.wait_ge(read_up.sem, here.at(read_up, i + f * PAIRS))
                        features(c, two(banks[4 if kind == "A" else 5]), in_hi, in_lo, DT)
                ffn_walk(pe, c0, step)

            def scores(here, h, q_ready):
                q_ready()
                rows = slice(HEAD_DIM * (h % 2), HEAD_DIM * (h % 2 + 1))
                for a in range(TT):
                    e = pe.matmul(banks[2 + h % 2][:, a, :], qk[rows, h // 2, a * P:(a + 1) * P],
                                  qk[rows, HALVES + h // 2, :], start=True, stop=True, skip_group_check=True)
                e.then_inc(scored.sem, 1)

            def turn_weights(here, h):
                pe.wait_ge(p_ready.sem, here.at(p_ready, h + 1))
                if h >= 1:
                    pe.wait_ge(pT_ready.sem, here.at(pT_ready, h))
                for k in range(TT):
                    for a in range(TT):
                        e = pe.transpose(banks[6][:, k, a * P:(a + 1) * P], soft[:, h % 2, a, k * P:(k + 1) * P], ident)
                e.then_inc(p_turned.sem, 1)

            def weigh_values(here, h):
                pe.wait_ge(pT_ready.sem, here.at(pT_ready, h + 1))
                j = h // 2
                if j >= 1:
                    pe.wait_ge(att_ready.sem, here.at(att_ready, j))
                rows = slice(HEAD_DIM * (h % 2), HEAD_DIM * (h % 2 + 1))
                for k in range(TT):
                    e = pe.matmul(banks[7][rows, j % 2, :], v_tok[:, k, h * HEAD_DIM:(h + 1) * HEAD_DIM],
                                  softT[:, h % 2, k, :], start=k == 0, stop=k == TT - 1, skip_group_check=True)
                e.then_inc(pv_done.sem, 1)

            pe.wait_ge(konst_in, 16)
            for j in range(HALVES):
                square_mean(None, 0, j)

            with pe.Fori(0, DEPTH) as layer:
                here = Place(0, layer)

                def normed(n):
                    def wait(k):
                        pe.wait_ge(xn_ready.sem, here.at(xn_ready, DT * n + k + 1))
                    return wait

                ffn(here, 0, 0, normed(0), gate_act, prod_ready, lambda j: square_mean(here, 0, j))
                for m in range(MIX1):
                    c = FFN_CHUNKS + m
                    bank = banks[4 + m % 2]
                    take(here, c)
                    if 2 <= m < 12:
                        pe.wait_ge(mix_evac.sem, here.at(mix_evac, m - 1))
                    elif m == 12:
                        pe.wait_ge(pool_ready.sem, here.at(pool_ready, 1))
                    elif m == 13:
                        pe.wait_ge(mix_evac.sem, here.at(mix_evac, 12))
                    elif m in (14, 15):
                        pe.wait_ge(branch_evac.sem, here.at(branch_evac, 2))
                    elif m in (16, 17):
                        pe.wait_ge(mix_evac.sem, here.at(mix_evac, m - 3))
                    elif m == 18:
                        pe.wait_ge(att_ready.sem, here.at(att_ready, HALVES))
                    elif m == 19:
                        pe.wait_ge(mix_evac.sem, here.at(mix_evac, 16))
                    if m == 0:
                        features(c, two(bank), in_hi, in_lo, DT, k_first=normed(1))
                    elif m in (4, 5):
                        tokens(c, bank, in_hi, in_lo)
                    elif m in (12, 13, 18, 19):
                        at = 4 * (m % 6 if m < 18 else m - 18)
                        outs = two(banks[at]) + two(banks[at + 1])
                        hi, lo = (br_hi, br_lo) if m < 18 else (att_hi, att_lo)
                        features(c, outs, hi, lo, HALVES)
                    elif m >= 20:
                        if m == 20:
                            pe.wait_ge(merged_lo.sem, here.at(merged_lo, 4))
                        features(c, two(banks[m - 20]), in_hi, in_lo, DT)
                        if m > 20:
                            square_mean(here, 1, m - 21)
                    else:
                        features(c, two(bank), in_hi, in_lo, DT)
                    if 1 <= m < 5:
                        p = m - 1
                        pe.wait_ge(qk_sq_ready.sem, here.at(qk_sq_ready, p + 1))
                        if p >= 1:
                            pe.wait_ge(qk_sd.sem, here.at(qk_sd, p))
                        pe.matmul(flat(banks[0][:, :, :]), head_mean, qk_sq[:, p % 2, :], start=True, stop=True
                                  ).then_inc(qk_ms.sem, 1)
                    if 2 <= m < 6:
                        p = m - 2
                        pe.wait_ge(qk_normed.sem, here.at(qk_normed, p + 1))
                        if p >= 1:
                            pe.wait_ge(qk_ready.sem, here.at(qk_ready, p))
                        pe.matmul(flat(banks[1][:, :, :]), rot1, flat(qk[:, 2 * p:2 * p + 2, :]), start=True, stop=True
                                  ).then_inc(qk_rot.sem, 1)
                    if m == 10:
                        pe.wait_ge(pool_d.sem, here.at(pool_d, 4))
                        pe.wait_ge(pool_w_ready.sem, here.at(pool_w_ready, 1))
                        for g in range(4):
                            e = pe.matmul(banks[g // 2][:, g % 2, :], pool_cur[:, g * P:(g + 1) * P], sums[g % 2][:, g, :],
                                          start=True, stop=True, skip_group_check=True)
                        e.then_inc(pool_y.sem, 1)
                    if 0 <= m - 7 < HEADS:
                        scores(here, m - 7, lambda: pe.wait_ge(qk_ready.sem, here.at(qk_ready, 4)))
                    if 0 <= m - 8 < HEADS:
                        turn_weights(here, m - 8)
                    if 0 <= m - 9 < HEADS:
                        weigh_values(here, m - 9)
                square_mean(here, 1, HALVES - 1)
                ffn(here, FFN_CHUNKS + MIX1, 1, normed(2), gate_act, prod_ready, lambda j: square_mean(here, 2, j))

            with pe.Fori(0, DEPTH) as layer:
                here = Place(1, layer)

                def mean(n, j):
                    pe.wait_ge(z_ready.sem, here.at(z_ready, HALVES * n + j + 1))
                    for f in (2 * j, 2 * j + 1):
                        e = pe.matmul(banks[6][:, 0, :], mean_of, x[:, f, :], start=f == 0, stop=f == DT - 1)
                    if j == HALVES - 1:
                        e.then_inc(mu_ready.sem, 1)

                def variance(n):
                    for f in range(DT):
                        pe.wait_ge(c_sq.sem, here.at(c_sq, DT * n + f + 1))
                        e = pe.matmul(banks[7][:, 0, :], mean_of, work[:, f, :], start=f == 0, stop=f == DT - 1)
                    e.then_inc(var_ready.sem, 1)

                def settled(n):
                    def wait(k):
                        pe.wait_ge(xs_ready.sem, here.at(xs_ready, DT * n + k + 1))
                    return wait

                for m in range(MIX2):
                    bank = banks[4 + m % 2]
                    take(here, m)
                    if 2 <= m < 22:
                        pe.wait_ge(mix_evac.sem, here.at(mix_evac, m - 1))
                    elif m == 22:
                        pe.wait_ge(ret_ready.sem, here.at(ret_ready, RET_HEADS))
                    elif m == 23:
                        pe.wait_ge(mix_evac.sem, here.at(mix_evac, 22))
                    elif m in (24, 25):
                        pe.wait_ge(branch_evac.sem, here.at(branch_evac, 2))
                    elif m in (26, 27):
                        pe.wait_ge(mix_evac.sem, here.at(mix_evac, m - 3))
                    elif m in (30, 31):
                        pe.wait_ge(branch_evac.sem, here.at(branch_evac, m - 27))
                    elif m == 36:
                        pe.wait_ge(mix_evac.sem, here.at(mix_evac, 26))
                        pe.wait_ge(ple_split.sem, here.at(ple_split, 1))
                    elif m in (38, 39):
                        pe.wait_ge(mix_evac.sem, here.at(mix_evac, 27))
                    elif m in (40, 41):
                        pe.wait_ge(mix_evac.sem, here.at(mix_evac, m - 11))
                    if m == 0:
                        features(m, two(bank), in_hi, in_lo, DT, k_first=settled(-1))
                    elif m in (4, 5) or 10 <= m < 14:
                        tokens(m, bank, in_hi, in_lo)
                    elif m in (22, 23):
                        at = 4 * (m - 22)
                        if m == 22:
                            pe.wait_ge(att_ready.sem, here.at(att_ready, HALVES))
                        features(m, two(banks[at]) + two(banks[at + 1]), att_hi, att_lo, HALVES)
                    elif 28 <= m < 32:
                        features(m, two(banks[m % 2]), br_hi, br_lo, DT)
                    elif 32 <= m < 36:
                        if m == 32:
                            pe.wait_ge(merged_lo.sem, here.at(merged_lo, 4))
                        features(m, two(banks[m - 32]), in_hi, in_lo, DT)
                        if m > 32:
                            mean(0, m - 33)
                        if m == 35:
                            mean(0, HALVES - 1)
                    elif m in (36, 37):
                        at = 4 if m == 36 else 2
                        features(m, two(banks[at]) + two(banks[at + 1]), ple_hi, ple_lo, 2)
                        if m == 36:
                            variance(0)
                    elif m == 38:
                        features(m, two(bank), in_hi, in_lo, DT, k_first=settled(0))
                    else:
                        features(m, two(bank), in_hi, in_lo, DT)
                    if 7 <= m < 11:
                        p = m - 7
                        pe.wait_ge(mix_evac.sem, here.at(mix_evac, 7 + p))
                        if p >= 2:
                            pe.wait_ge(qk_ready.sem, here.at(qk_ready, p - 1))
                        pe.matmul(flat(banks[p % 2][:, :, :]), rot2, flat(ret_qk[:, 2 * p:2 * p + 2, :]), start=True,
                                  stop=True).then_inc(qk_rot.sem, 1)
                    if 0 <= m - 5 < HEADS:
                        scores(here, m - 5, lambda: pe.wait_ge(mix_evac.sem, here.at(mix_evac, 4)))
                    if 0 <= m - 6 < HEADS:
                        turn_weights(here, m - 6)
                    if 0 <= m - 7 < HEADS:
                        weigh_values(here, m - 7)
                    if 0 <= m - 15 < RET_HEADS:
                        h = m - 15
                        pe.wait_ge(qk_ready.sem, here.at(qk_ready, 4))
                        if h >= 2:
                            pe.wait_ge(ret_p.sem, here.at(ret_p, h - 1))
                        for a in range(TT):
                            e = pe.matmul(banks[2 + h % 2][:, a, :], ret_qk[:, RET_HEADS + h, a * P:(a + 1) * P],
                                          ret_qk[:, h, :], start=True, stop=True, skip_group_check=True)
                        e.then_inc(ret_scored.sem, 1)
                    if 0 <= m - 16 < RET_HEADS:
                        h = m - 16
                        pe.wait_ge(ret_p.sem, here.at(ret_p, h + 1))
                        if h >= 2:
                            pe.wait_ge(ret_o.sem, here.at(ret_o, h - 1))
                        for a in range(TT):
                            for k in range(TT):
                                e = pe.matmul(banks[h % 2][:, a, :], softT[:, h % 2, k, a * P:(a + 1) * P],
                                              ret_v[:, k, h * RET_V:(h + 1) * RET_V], start=k == 0, stop=k == TT - 1,
                                              skip_group_check=True)
                        e.then_inc(ret_pv.sem, 1)
                    if 0 <= m - 18 < RET_HEADS:
                        h = m - 18
                        pe.wait_ge(ret_o.sem, here.at(ret_o, h + 1))
                        if h >= 1:
                            pe.wait_ge(ret_y.sem, here.at(ret_y, h))
                        for f in range(2):
                            for a in range(TT):
                                e = pe.transpose(banks[6][:, f, a * P:(a + 1) * P], soft[:, h % 2, a, f * P:(f + 1) * P], ident)
                        e.then_inc(ret_turned.sem, 1)

                def up_bank(k):
                    if k == 0:
                        pe.wait_ge(mix_evac.sem, here.at(mix_evac, 32))
                ffn(here, MIX2, 0, up_bank, gate_taps, up_taps, lambda j: mean(1, j))
                variance(1)
    return nc


def _constants():
    f32 = np.float32
    k = np.zeros((P, CONSTS), f32)
    k[:, K_IDENT:K_IDENT + P] = np.eye(P)
    k[:, K_MEAN:K_MEAN + P] = 1.0 / D
    p = np.arange(P)
    k[:, K_HEAD:K_HEAD + P] = (p[:, None] // HEAD_DIM == p[None, :] // HEAD_DIM) / HEAD_DIM
    t = np.arange(T, dtype=f32)
    for half, rot, cos, sin in ((HEAD_DIM // 2, K_ROT1, K_COS1, K_SIN1), (RET_QK // 2, K_ROT2, K_COS2, K_SIN2)):
        low = p % (2 * half) < half
        k[np.where(low, p + half, p - half), rot + p] = np.where(low, -1.0, 1.0)
        j = np.arange(half, dtype=f32)
        if half == HEAD_DIM // 2:
            inv = (f32(1.0) / (f32(ROPE_BASE) ** (j * f32(2.0 / HEAD_DIM)))).astype(f32)
        else:
            inv = (f32(ROPE_BASE) ** (-j / f32(half))).astype(f32)
        angle = (t[None, :] * inv[p % half][:, None]).astype(f32).astype(np.float64)
        k[:, cos:cos + T] = np.cos(angle)
        k[:, sin:sin + T] = np.sin(angle)
    for a in range(TT):
        query = a * P + p[:, None]
        k[:, K_CAUSAL + a * T:K_CAUSAL + (a + 1) * T] = np.where(np.arange(T)[None, :] <= query, 0.0, NEG)
        k[:, K_DIST + a * T:K_DIST + (a + 1) * T] = np.arange(T)[None, :] - query
    col = p % GRID_W
    start = np.clip(col - NA_COLS // 2, 0, GRID_W - NA_COLS)[:, None]
    key = np.arange(GRID_W)[None, :]
    k[:, K_WIN:K_WIN + GRID_W] = np.where((key >= start) & (key < start + NA_COLS), 0.0, NEG)
    for g, w in enumerate(WINDOWS):
        n = np.arange(POOL_EDGE)
        k[:, K_EDGE + g * POOL_EDGE:K_EDGE + (g + 1) * POOL_EDGE] = w / np.minimum(n + 1, w)
    return k


def _tile(w, rows, cols):
    part = w[rows, cols]
    return part.reshape(-1, P, part.shape[1]).transpose(1, 0, 2).reshape(P, -1)


def _ffn_chunks(up, down):
    whole = slice(None)

    def piece(kind, i):
        if kind == "D":
            return _tile(down, slice(i * T, (i + 1) * T), whole)
        at = i * T + (D_FF if kind == "B" else 0)
        return _tile(up, whole, slice(at, at + T))

    order = [("A", 0), ("B", 0)]
    for i in range(1, PAIRS):
        order += [("A", i), ("B", i), ("D", i - 1)]
    return [piece(*o) for o in order + [("D", PAIRS - 1)]]


def _columns(w, n, first=0):
    return [_tile(w, slice(None), slice(first + i * T, first + (i + 1) * T)) for i in range(n)]


def _stream(a):
    chunks = []
    for l in range(DEPTH):
        w, wide = a["w_in"][l], 4 * P
        chunks += _ffn_chunks(a["ffn1_w_gate_up"][l], a["ffn1_w_down"][l])
        chunks += _columns(w, 6, 512) + _columns(w, 2) + _columns(w, 4, 2048)
        chunks += [_tile(a["w_branch_pool"][l], slice(None), slice(i * wide, (i + 1) * wide)) for i in range(2)]
        chunks += _columns(w, 4, 3072)
        chunks += [_tile(a["w_branch_attn"][l], slice(None), slice(i * wide, (i + 1) * wide)) for i in range(2)]
        chunks += _columns(a["w_out"][l], 4)
        chunks += _ffn_chunks(a["ffn2_w_gate_up"][l], a["ffn2_w_down"][l])
    for l in range(DEPTH):
        w = a["w_in_2"][l]
        chunks += _columns(w, 22)
        chunks += [_tile(a["w_branch_a_2"][l], slice(None), slice(i * wide, (i + 1) * wide)) for i in range(2)]
        chunks += _columns(w, 4, 22 * T)
        chunks += _columns(a["w_branch_b_2"][l], 4) + _columns(a["w_out_2"][l], 4)
        for i in range(2):
            half = np.zeros((P, CHUNK), np.float32)
            half[:, :CHUNK // 2] = _tile(a["w_ple_proj_2"][l], slice(None), slice(i * wide, (i + 1) * wide))
            chunks.append(half)
        chunks += _columns(a["w_ple_gate_2"][l], 4)
        chunks += _ffn_chunks(a["w_up_2"][l], a["w_down_2"][l])
    out = np.empty((STREAM, P, CHUNK), np.float32)
    for n, c in enumerate(chunks):
        out[n] = c
    assert len(chunks) == STREAM
    return out


def _col(v):
    return v.reshape(-1, P).T


def kernel(**inputs):
    import concourse.bacc as bacc
    from concourse.bass_utils import run_bass_kernel_spmd

    a = {k: np.ascontiguousarray(v) for k, v in inputs.items()}
    cols1 = np.concatenate([np.concatenate(
        [_col(a[n][l]) for n in ("ffn1_norm", "mix_norm", "ffn2_norm", "b_gate", "pool_scale")]
        + [np.concatenate([a[n][l], a[n][l]])[:, None] for n in ("q_norm", "k_norm")], axis=1)
        for l in range(DEPTH)], axis=1)
    cols2 = np.concatenate([np.concatenate(
        [_col(a[n][l]) for n in ("ln1_g_2", "ln1_b_2", "ln2_g_2", "ln2_b_2")]
        + [_col(a["conv_w_2"][l][tap]) for tap in range(3)] + [_col(a["conv_b_2"][l])]
        + [np.tile(a[n][l][None, :], (P, 1)) for n in ("ret_decay_f_2", "ret_decay_b_2")], axis=1)
        for l in range(DEPTH)], axis=1)
    q_row, q_col = (np.arange(P) // GRID_W)[:, None, None], (np.arange(P) % GRID_W)[:, None, None]
    step = np.arange(ROW_STEPS)[None, :, None] - (TT - 1) * (P // GRID_W)
    entry = (step - q_row + NA_ROWS - 1) * (2 * NA_COLS - 1) + np.arange(GRID_W)[None, None, :] - q_col + NA_COLS - 1
    rpb = a["na_rpb_2"].reshape(DEPTH, HEADS, -1)[:, :, entry].transpose(0, 2, 1, 3, 4).reshape(DEPTH, P, -1)
    arrays = {
        "xT": _tile(a["x"][0].T, slice(None), slice(None)),
        "stream": _stream(a),
        "cols1": cols1,
        "cols2": cols2,
        "pool_w": a["pool_w"].transpose(2, 0, 1, 3).reshape(P, -1),
        "pT": np.stack([_tile(a["p_2"][l, 0].T, slice(None), slice(None)) for l in range(DEPTH)]),
        "rpb": rpb,
        "consts": _constants(),
    }
    arrays = {k: np.ascontiguousarray(v) for k, v in arrays.items()}
    nc = bacc.Bacc("TRN2", target_bir_lowering=False, num_devices=1)
    args = [nc.dram_tensor(k, v.shape, F32, kind="ExternalInput").ap() for k, v in arrays.items()]
    args.append(nc.dram_tensor("result", (P, DT * T), F32, kind="ExternalOutput").ap())
    hybrid_and_neighbourhood_kernel(nc, *args)
    r = run_bass_kernel_spmd(nc, [arrays], core_ids=[0])
    got = r.results[0]["result"]
    return np.ascontiguousarray(got.reshape(P, DT, T).transpose(2, 1, 0).reshape(1, T, D))
```

```python
from contextlib import ExitStack

import numpy as np

import concourse.bass as bass
from concourse import mybir

F32 = mybir.dt.float32
F32R = mybir.dt.float32r
ACT = mybir.ActivationFunctionType
ALU = mybir.AluOpType

P = 128
T = 256
D = 1024
DT = D // P
TT = T // P
DEPTH = 2
D_FF = 2816
PAIRS = D_FF // T
HEADS, HEAD_DIM = 8, 64
HALVES = HEADS // 2
WINDOWS = (2, 4, 8, 16)
POOL_EDGE = max(WINDOWS)
RET_HEADS, RET_QK, RET_V = 4, 128, 256
GRID_W, NA_ROWS, NA_COLS = 64, 8, 16
GRID_ROWS = T // GRID_W
ROW_STEPS = GRID_ROWS + P // GRID_W
ROPE_BASE = 10000.0
EPS, LN_EPS, GN_EPS = 1e-6, 1e-5, 1e-6
ALPHA = (2.0 * DEPTH) ** 0.25
NEG = -1e30
LOWEST = float(np.finfo(np.float32).min)

CAUSAL_KEYS = tuple((a + 1) * P for a in range(TT))
ALL_KEYS = (T,) * TT

TURN = (HEAD_DIM // 2, RET_QK // 2)

SLOTS = 3
CHUNK = 2048
FFN_CHUNKS = 3 * PAIRS
MIX1 = 24
MIX2 = 42
CHUNKS = (2 * FFN_CHUNKS + MIX1, MIX2 + FFN_CHUNKS)
USES = tuple(c // SLOTS for c in CHUNKS)
STREAM = DEPTH * sum(CHUNKS)
SMALL = 4 + len(WINDOWS)

C_FFN1, C_MIX, C_FFN2, C_GATE, C_SCALE, C_Q, C_K = 0, 8, 16, 24, 40, 44, 45
COLS1 = 46
FT = 2 * D_FF // P
C_G1, C_B1, C_G2, C_B2, C_TAP, C_CONVB = 0, 8, 16, 24, 32, 32 + 3 * FT
C_LF = C_CONVB + FT
C_LB = C_LF + RET_HEADS
COLS2 = C_LB + RET_HEADS

K_IDENT, K_MEAN, K_HEAD = 0, P, 2 * P
K_COS1 = 3 * P
K_SIN1, K_COS2, K_SIN2 = K_COS1 + T, K_COS1 + 2 * T, K_COS1 + 3 * T
K_CAUSAL = K_COS1 + 4 * T
K_DIST = K_CAUSAL + TT * T
K_WIN = K_DIST + 2 * TT * T
K_EDGE = K_WIN + GRID_W
CONSTS = K_EDGE + len(WINDOWS) * POOL_EDGE


class Signal:

    def __init__(self, sem, hybrid, second=0, setup=0, between=0):
        self.sem = sem
        self.per = (hybrid, second)
        self.before = (setup, setup + DEPTH * hybrid + between)


class Place:

    def __init__(self, kind, layer):
        self.kind, self.layer = kind, layer

    def at(self, signal, n):
        return self.layer * signal.per[self.kind] + (signal.before[self.kind] + n)

    def uses(self, c, turn=0):
        return self.layer * USES[self.kind] + (self.kind * DEPTH * USES[0] + c // SLOTS) + turn


def ffn_walk(eng, c0, step):
    for n, (kind, i) in enumerate((("A", 0), ("B", 0), ("A", 1), ("B", 1), ("D", 0))):
        step(kind, i, c0 + n, 0)
    with eng.Fori(0, PAIRS - 3) as turn:
        for n, (kind, lag) in enumerate((("A", 0), ("B", 0), ("D", 1))):
            step(kind, turn + (2 - lag), c0 + 5 + n, turn)
    for n, (kind, lag) in enumerate((("A", 0), ("B", 0), ("D", 1))):
        step(kind, PAIRS - 1 - lag, c0 + FFN_CHUNKS - 4 + n, 0)
    step("D", PAIRS - 1, c0 + FFN_CHUNKS - 1, 0)


def hybrid_and_neighbourhood_kernel(nc, xT, stream, cols1, cols2, pool_w, pT, rpb, consts, out):
    ctx = ExitStack()
    with ctx:
        def sb(name, shape, dt=F32):
            return ctx.enter_context(nc.sbuf_tensor(name, shape, dt))

        def sem(name):
            return ctx.enter_context(nc.semaphore(name))

        def signal(name, hybrid, second=0, setup=0, between=0):
            return Signal(sem(name), hybrid, second, setup, between)

        raw = sb("raw", [P, SLOTS, CHUNK])
        w_hi = sb("w_hi", [P, SLOTS, CHUNK], F32R)
        w_lo = sb("w_lo", [P, SLOTS, CHUNK], F32R)
        x = sb("x", [P, DT, T])
        in_hi = sb("in_hi", [P, DT, T], F32R)
        in_lo = sb("in_lo", [P, DT, T], F32R)
        att_hi = sb("att_hi", [P, HALVES, T], F32R)
        att_lo = sb("att_lo", [P, HALVES, T], F32R)
        br_hi = sb("br_hi", [P, DT, T], F32R)
        br_lo = sb("br_lo", [P, DT, T], F32R)
        hid_hi = sb("hid_hi", [P, 2, T], F32R)
        hid_lo = sb("hid_lo", [P, 2, T], F32R)
        ple_hi = sb("ple_hi", [P, 2, T], F32R)
        ple_lo = sb("ple_lo", [P, 2, T], F32R)
        konst = sb("konst", [P, CONSTS])
        col1 = sb("col1", [P, DEPTH + 1, COLS1])
        col2 = sb("col2", [P, DEPTH, COLS2])
        cur = sb("cur", [P, COLS2])
        gain1 = sb("gain1", [P, DT])
        small = sb("small", [P, 8])
        eps6, eps5, minus_half, floor0 = small[:, 0:1], small[:, 1:2], small[:, 2:3], small[:, 7:8]
        decay = sb("decay", [P, 4, DEPTH * 2 * RET_HEADS])
        ms = sb("ms", [P, TT])
        rs = sb("rs", [P, TT])
        floor = sb("floor", [P, TT])
        qk_var = sb("qk_var", [P, TT, 2 * HEADS])
        qk_rs = sb("qk_rs", [P, TT, 2 * HEADS])
        k_cols = sb("k_cols", [P, TT, 2 * P])
        weigh = sb("weigh", [P, TT, P])
        stat = sb("stat", [P, 2, 8])
        group = sb("group", [P, 2, TT, 12])
        soft = sb("soft", [P, 2, TT, T])
        softT = sb("softT", [P, 2, TT, T])
        ple_in = sb("ple_in", [P, 2, T])

        ret_turn2 = sb("ret_turn2", [P, 2, T])

        area0 = sb("area0", [P, DT, T])
        area1 = sb("area1", [P, TT, 2 * T])
        area2 = sb("area2", [P, DT, T])
        area3 = sb("area3", [P, DT, T])
        area4 = sb("area4", [P, HEADS * ROW_STEPS * GRID_W])
        area5 = sb("area5", [P, DT, T])
        work = area0
        work_of = (area0, area2, area0, area0)
        qk = area0
        v_tok = area1
        gates1 = (area2, area3)
        gates2 = area0
        merged1, merged2 = area2, area2
        glu_a = area2[:, 0:2, :]
        glu_b = area2[:, 2:4, :]
        hidden = area2[:, 4:6, :]
        u = area4[:, 0:4 * T].rearrange("p (g t) -> p g t", g=4)
        sums = [area4[:, (1 + b) * 4 * T:(2 + b) * 4 * T].rearrange("p (g t) -> p g t", g=4) for b in (0, 1)]
        pool_both = area5[:, 0:4, :].rearrange("p a t -> p (a t)")
        pool_cur = area5[:, 4:6, :].rearrange("p a t -> p (a t)")
        qk_sq = area3[:, 0:4, :].rearrange("p (b a) t -> p b (a t)", b=2)
        silu_g = area4[:, 0:DT * T].rearrange("p (f t) -> p f t", f=DT)
        ret_qk = area2
        ret_v = area3[:, :, :].rearrange("p f t -> p (f t)").rearrange("p (a n) -> p a n", a=TT)
        ret_turn = ret_v[:, :, 3 * T:4 * T]
        ple_out = area3
        ple_gate = area1
        turned_places = ((softT[:, 0, :, :], softT[:, 1, :, :]), (ret_turn, ret_turn2[:, :, :]))
        backward = area3[:, :, :].rearrange("p (h m) t -> p h (m t)", h=RET_HEADS)
        z_pairs = area5[:, 0:2, :]
        decays = area5[:, :, :].rearrange("p (h m) t -> p h (m t)", h=RET_HEADS)

        banks = [ctx.enter_context(nc.psum_tensor(f"bank{b}", [P, 2, T], F32)) for b in range(8)]
        rstd_norm, rstd_ln = banks[6][:, 1, :], banks[7][:, 1, :]

        def flat(ap):
            return ap.rearrange("p a t -> p (a t)")

        ident = konst[:, K_IDENT:K_IDENT + P]
        mean_of = konst[:, K_MEAN:K_MEAN + P]
        head_mean = konst[:, K_HEAD:K_HEAD + P:HEAD_DIM]

        def table(k):
            return konst[:, k:k + T].unsqueeze(1).broadcast_to([P, 2, T])

        causal = konst[:, K_CAUSAL:K_CAUSAL + TT * T].rearrange("p (a t) -> p a t", a=TT)
        later = konst[:, K_DIST:K_DIST + TT * T]
        earlier = konst[:, K_DIST + TT * T:K_DIST + 2 * TT * T]
        window = konst[:, K_WIN:K_WIN + GRID_W]
        edge = konst[:, K_EDGE:CONSTS].rearrange("p (g t) -> p g t", g=len(WINDOWS))

        raw_full = [sem(f"raw_full{s}") for s in range(SLOTS)]
        hi_ready = [sem(f"hi_ready{s}") for s in range(SLOTS)]
        lo_ready = [sem(f"lo_ready{s}") for s in range(SLOTS)]
        w_used = [sem(f"w_used{s}") for s in range(SLOTS)]
        x_in = [sem(f"x_in{j}") for j in range(HALVES)]
        col1_in, col2_in = sem("col1_in"), sem("col2_in")
        matrices_in, konst_in = sem("matrices_in"), sem("konst_in")
        small_set = sem("small_set")
        out_done = sem("out_done")
        decay_step, decay_scal = sem("decay_step"), sem("decay_scal")
        cur_ready = signal("cur_ready", 1, 1)
        x_ready = signal("x_ready", 3 * HALVES, setup=HALVES)
        gain_ready = signal("gain_ready", 1, setup=1)
        xg_hi = signal("xg_hi", 3 * DT, setup=DT)
        xg_ready = signal("xg_ready", 3 * DT, setup=DT)
        sq_ready = signal("sq_ready", 3 * HALVES, setup=HALVES)
        sq_sum = signal("sq_sum", 3 * (HALVES - 1))
        ss_ready = signal("ss_ready", 3)
        ms_ready = signal("ms_ready", 3)
        rs_ready = signal("rs_ready", 3)
        rstd_ready = signal("rstd_ready", 3)
        xnf_ready = signal("xnf_ready", 3 * DT)
        xn_hi = signal("xn_hi", 3 * DT)
        xn_ready = signal("xn_ready", 3 * DT)
        gate_out = signal("gate_out", 2)
        gate_scaled = signal("gate_scaled", 4)
        gate_act = signal("gate_act", 2 * PAIRS, PAIRS)
        gate_left = signal("gate_left", 0, PAIRS)
        gate_taps = signal("gate_taps", 0, PAIRS)
        gelu_ready = signal("gelu_ready", 0, PAIRS)
        up_mid = signal("up_mid", 0, PAIRS)
        up_left = signal("up_left", 0, PAIRS)
        up_taps = signal("up_taps", 0, PAIRS)
        prod_ready = signal("prod_ready", 2 * PAIRS, PAIRS)
        hid_hi_ready = signal("hid_hi_ready", 2 * PAIRS, PAIRS)
        hid_ready = signal("hid_ready", 2 * PAIRS, PAIRS)
        acc_done = signal("acc_done", 2 * (HALVES - 1), HALVES - 1)
        mix_evac = signal("mix_evac", 16, 32)
        branch_evac = signal("branch_evac", 2, 6)
        qk_sq_ready = signal("qk_sq_ready", 4)
        qk_ms = signal("qk_ms", 4)
        qk_var_ready = signal("qk_var_ready", 4)
        qk_rs_ready = signal("qk_rs_ready", 4)
        k_cols_ready = signal("k_cols_ready", 2)
        k_spread = signal("k_spread", 2)
        k_normed = signal("k_normed", 2)
        qk_turned = [signal(f"qk_turned{b}", *(2 * 16 * P // half for half in TURN)) for b in range(2)]
        qk_sin = signal("qk_sin", 4, 4)
        qk_cos = signal("qk_cos", 4, 4)
        qk_ready = signal("qk_ready", 4, 4)
        pool_step = signal("pool_step", 14)
        pool_d = signal("pool_d", len(WINDOWS))
        pool_w_ready = signal("pool_w_ready", 1)
        pool_in = sem("pool_in")
        pool_y = signal("pool_y", 1)
        pool_hi = signal("pool_hi", 4)
        pool_ready = signal("pool_ready", 1)
        sig_ready = signal("sig_ready", 2)
        attn_pair = signal("attn_pair", 1)
        part_ready = signal("part_ready", 4, 8)
        merged_ready = signal("merged_ready", 4, 4)
        merged_hi = signal("merged_hi", 4, 4)
        merged_lo = signal("merged_lo", 4, 4)
        scored = signal("scored", HEADS, HEADS)
        max_ready = signal("max_ready", HEADS, HEADS)
        nmax_ready = signal("nmax_ready", HEADS, HEADS)
        exp_ready = signal("exp_ready", HEADS, HEADS)
        inv_ready = signal("inv_ready", HEADS, HEADS)
        weigh_ready = signal("weigh_ready", HEADS, HEADS)
        p_turned = signal("p_turned", HEADS, HEADS)
        pT_ready = signal("pT_ready", HEADS, HEADS)
        pv_done = signal("pv_done", HEADS, HEADS)
        att_hi_ready = signal("att_hi_ready", HALVES, HALVES)
        att_ready = signal("att_ready", HALVES, HALVES)
        xs_hi = signal("xs_hi", 0, 2 * DT, between=DT)
        xs_ready = signal("xs_ready", 0, 2 * DT, between=DT)
        bias_in = sem("bias_in")
        ple_in_sem = sem("ple_in_sem")
        bias_ready = signal("bias_ready", 0, 1)
        dist_step = signal("dist_step", 0, 2 * RET_HEADS)
        dist_ready = signal("dist_ready", 0, RET_HEADS)
        decay_ready = signal("decay_ready", 0, RET_HEADS)
        ret_scored = signal("ret_scored", 0, RET_HEADS)
        ret_p = signal("ret_p", 0, RET_HEADS)
        ret_pv = signal("ret_pv", 0, RET_HEADS)
        ret_stats = signal("ret_stats", 0, RET_HEADS)
        ret_mv = signal("ret_mv", 0, RET_HEADS)
        ret_var = signal("ret_var", 0, RET_HEADS)
        ret_rstd = signal("ret_rstd", 0, RET_HEADS)
        ret_o = signal("ret_o", 0, RET_HEADS)
        ret_turned = signal("ret_turned", 0, RET_HEADS)
        ret_y = signal("ret_y", 0, RET_HEADS)
        ret_hi = signal("ret_hi", 0, RET_HEADS)
        ret_ready = signal("ret_ready", 0, RET_HEADS)
        ple_split_hi = signal("ple_split_hi", 0, 1)
        ple_split = signal("ple_split", 0, 1)
        ple_mul = signal("ple_mul", 0, 4)
        base_ready = signal("base_ready", 0, 4)
        z_ready = signal("z_ready", 0, 2 * HALVES)
        z_sum = signal("z_sum", 0, 4)
        mu_ready = signal("mu_ready", 0, 2)
        c_ready = signal("c_ready", 0, 2 * DT)
        c_sq = signal("c_sq", 0, 2 * DT)
        var_ready = signal("var_ready", 0, 2)
        ln_var = signal("ln_var", 0, 2)
        ln_rs = signal("ln_rs", 0, 2)
        ln_rstd = signal("ln_rstd", 0, 2)
        ln_scaled = signal("ln_scaled", 0, 2 * DT)
        x_new = signal("x_new", 0, 2 * DT)

        block = ctx.enter_context(nc.Block())

        @block.sync
        def _(sp):
            sp.dma_start(col1[:, :, :].rearrange("p l c -> p (l c)"), cols1).then_inc(col1_in, 16)
            for j in range(HALVES):
                sp.dma_start(flat(x[:, 2 * j:2 * j + 2, :]), xT[:, j * 2 * T:(j + 1) * 2 * T]).then_inc(x_in[j], 16)
            for s in range(SLOTS):
                sp.dma_start(raw[:, s, :], stream[s]).then_inc(raw_full[s], 16)
                if s == 0:
                    sp.dma_start(konst[:, 0:K_COS1], consts[:, 0:K_COS1]).then_inc(matrices_in, 16)
            sp.dma_start(konst[:, K_COS1:CONSTS], consts[:, K_COS1:CONSTS]).then_inc(konst_in, 16)
            sp.dma_start(col2[:, :, :].rearrange("p l c -> p (l c)"), cols2).then_inc(col2_in, 16)
            with sp.Fori(1, STREAM // SLOTS) as n:
                for s in range(SLOTS):
                    sp.wait_ge(lo_ready[s], n)
                    sp.dma_start(raw[:, s, :], stream[bass.ds(n * SLOTS + s, 1)].rearrange("a p n -> (a p) n")
                                 ).then_inc(raw_full[s], 16)
            for j in range(HALVES):
                sp.wait_ge(x_new.sem, (2 * DEPTH - 1) * DT + 2 * j + 2)
                sp.dma_start(out[:, j * 2 * T:(j + 1) * 2 * T], flat(x[:, 2 * j:2 * j + 2, :])).then_inc(out_done, 16)
            sp.wait_ge(out_done, HALVES * 16)

        @block.gpsimd
        def _(pool):
            pool.memset(eps6, EPS).then_inc(small_set, 1)
            pool.memset(eps5, LN_EPS).then_inc(small_set, 1)
            pool.memset(minus_half, -0.5).then_inc(small_set, 1)
            for g, w in enumerate(WINDOWS):
                pool.memset(small[:, 3 + g:4 + g], 1.0 / w).then_inc(small_set, 1)
            pool.memset(floor0, HEAD_DIM * EPS * EPS).then_inc(small_set, 1)
            pool.wait_ge(small_set, SMALL)
            pool.wait_ge(raw_full[2], 16)
            pool.dma_start(pool_both, pool_w).then_inc(pool_in, 16)

            def power(out, base):
                return pool.tensor_tensor(out, base, minus_half.unsqueeze(1).broadcast_to([P, *base.shape[1:]])
                                          if len(base.shape) > 2 else minus_half.broadcast_to([P, TT]), ALU.pow)

            def rest(out, whole, upper):
                return pool.tensor_tensor(out, whole, upper.bitcast(F32), ALU.subtract)

            def norm(here, n):
                pool.wait_ge(ms_ready.sem, here.at(ms_ready, n + 1))
                power(rs[:, :], ms[:, :]).then_inc(rs_ready.sem, 1)
                for k in range(DT):
                    pool.wait_ge(xn_hi.sem, here.at(xn_hi, DT * n + k + 1))
                    rest(in_lo[:, k, :], work_of[n][:, k, :], in_hi[:, k, :]).then_inc(xn_ready.sem, 1)

            def merged_lower(here, merged, upper, lower):
                for j in range(HALVES):
                    pool.wait_ge(merged_hi.sem, here.at(merged_hi, j + 1))
                    rest(lower[:, 2 * j:2 * j + 2, :], merged[:, 2 * j:2 * j + 2, :], upper[:, 2 * j:2 * j + 2, :]
                         ).then_inc(merged_lo.sem, 1)

            def layer_norm(here, n):
                for j in (1, 2):
                    pool.wait_ge(z_ready.sem, here.at(z_ready, HALVES * n + j + 1))
                    if j == 2:
                        pool.wait_ge(z_sum.sem, here.at(z_sum, 2 * n + 1))
                    pool.tensor_tensor(z_pairs, x[:, 0:2, :] if j == 1 else z_pairs, x[:, 2 * j:2 * j + 2, :], ALU.add
                                       ).then_inc(z_sum.sem, 1)
                pool.wait_ge(ln_var.sem, here.at(ln_var, n + 1))
                power(rs[:, :], ms[:, :]).then_inc(ln_rs.sem, 1)
                for k in range(DT):
                    pool.wait_ge(xs_hi.sem, here.at(xs_hi, DT * n + k + 1))
                    rest(br_lo[:, k, :], x[:, k, :], br_hi[:, k, :]).then_inc(xs_ready.sem, 1)

            def sum_squares(here, n):
                first = work_of[n][:, 0:2, :]
                for j in range(1, HALVES):
                    pool.wait_ge(sq_ready.sem, here.at(sq_ready, HALVES * (n - 1) + j + 1))
                    if j >= 2:
                        pool.wait_ge(sq_sum.sem, here.at(sq_sum, (HALVES - 1) * n + j - 1))
                    pool.tensor_tensor(first, first, work_of[n][:, 2 * j:2 * j + 2, :], ALU.add).then_inc(sq_sum.sem, 1)

            with pool.Fori(0, DEPTH) as layer:
                here = Place(0, layer)
                sum_squares(here, 0)
                norm(here, 0)
                sum_squares(here, 1)
                norm(here, 1)
                for p in range(HALVES):
                    pool.wait_ge(qk_var_ready.sem, here.at(qk_var_ready, p + 1))
                    power(qk_rs[:, :, 4 * p:4 * p + 4], qk_var[:, :, 4 * p:4 * p + 4]).then_inc(qk_rs_ready.sem, 1)
                pool.wait_ge(konst_in, 16)
                pool.wait_ge(pool_in, 16)
                pool.wait_ge(mix_evac.sem, here.at(mix_evac, 8))
                for k in range(len(WINDOWS)):
                    back = 2 ** k
                    src = u if k == 0 else sums[(k - 1) % 2]
                    if k:
                        pool.wait_ge(pool_step.sem, here.at(pool_step, 2 * k))
                    pool.tensor_tensor(sums[k % 2][:, k:4, back:T], src[:, k:4, back:T], src[:, k:4, 0:T - back],
                                       ALU.add).then_inc(pool_step.sem, 1)
                    pool.tensor_copy(sums[k % 2][:, k:4, 0:back], src[:, k:4, 0:back]).then_inc(pool_step.sem, 1)
                pool.tensor_copy(pool_cur, pool_both[:, bass.ds(layer * (4 * P), 4 * P)]).then_inc(pool_w_ready.sem, 1)
                pool.wait_ge(pool_step.sem, here.at(pool_step, 8))
                for b in range(2):
                    first = sums[b][:, b:4:2, 0:POOL_EDGE]
                    pool.tensor_tensor(first, first, edge[:, b:4:2, :], ALU.mult).then_inc(pool_step.sem, 1)
                pool.wait_ge(pool_step.sem, here.at(pool_step, 10))
                for g in range(len(WINDOWS)):
                    pool.tensor_tensor(sums[g % 2][:, g, :], sums[g % 2][:, g, :],
                                       small[:, 3 + g:4 + g].broadcast_to([P, T]), ALU.mult).then_inc(pool_step.sem, 1)
                for g in range(len(WINDOWS)):
                    pool.wait_ge(pool_step.sem, here.at(pool_step, 11 + g))
                    pool.tensor_tensor(sums[g % 2][:, g, :], sums[g % 2][:, g, :], u[:, g, :], ALU.subtract
                                       ).then_inc(pool_d.sem, 1)
                merged_lower(here, merged1, in_hi, in_lo)
                sum_squares(here, 2)
                norm(here, 2)

            def load_tables(l, n):
                pool.dma_start(area4[:, :], rpb[bass.ds(l, 1)].rearrange("a p n -> (a p) n")).then_inc(bias_in, 16)
                pool.dma_start(flat(ple_in[:, :, :]), pT[bass.ds(l, 1)].rearrange("a p n -> (a p) n")
                               ).then_inc(ple_in_sem, 16)
                pool.wait_ge(bias_in, n * 16)
                masks = window.unsqueeze(1).broadcast_to([P, HEADS * ROW_STEPS, GRID_W])
                rows = area4[:, :].rearrange("p (m c) -> p m c", c=GRID_W)
                pool.tensor_tensor(rows, rows, masks, ALU.add).then_inc(bias_ready.sem, 1)

            pool.wait_ge(pool_y.sem, DEPTH)
            load_tables(0, 1)
            with pool.Fori(0, DEPTH) as layer:
                here = Place(1, layer)
                pool.wait_ge(xs_ready.sem, here.at(xs_ready, 0))
                pool.wait_ge(cur_ready.sem, here.at(cur_ready, 1))
                for h in range(RET_HEADS):
                    pool.tensor_tensor(decays[:, h, :], later, cur[:, C_LF + h:C_LF + h + 1].broadcast_to([P, TT * T]),
                                       ALU.mult).then_inc(dist_step.sem, 1)
                    pool.tensor_tensor(backward[:, h, :], earlier, cur[:, C_LB + h:C_LB + h + 1].broadcast_to([P, TT * T]),
                                       ALU.mult).then_inc(dist_step.sem, 1)
                pool.wait_ge(dist_step.sem, here.at(dist_step, 2 * RET_HEADS))
                for h in range(RET_HEADS):
                    pool.tensor_tensor(decays[:, h, :], decays[:, h, :], backward[:, h, :], ALU.add
                                       ).then_inc(dist_ready.sem, 1)
                for n in range(RET_HEADS + 2):
                    if n < RET_HEADS:
                        h = n
                        pool.wait_ge(ret_var.sem, here.at(ret_var, h + 1))
                        power(group[:, h % 2, :, 11:12], group[:, h % 2, :, 10:11]).then_inc(ret_rstd.sem, 1)
                    if n >= 2:
                        h = n - 2
                        pool.wait_ge(ret_hi.sem, here.at(ret_hi, h + 1))
                        rest(in_lo[:, 2 * h:2 * h + 2, :], silu_g[:, 2 * h:2 * h + 2, :], in_hi[:, 2 * h:2 * h + 2, :]
                             ).then_inc(ret_ready.sem, 1)
                pool.wait_ge(ple_split_hi.sem, here.at(ple_split_hi, 1))
                rest(ple_lo[:, :, :], ple_in[:, :, :], ple_hi[:, :, :]).then_inc(ple_split.sem, 1)
                merged_lower(here, merged2, br_hi, br_lo)
                pool.wait_ge(ret_ready.sem, here.at(ret_ready, RET_HEADS))
                pool.wait_ge(ple_split.sem, here.at(ple_split, 1))
                layer_norm(here, 0)
                with pool.If(layer < DEPTH - 1):
                    following = nc.s_assert_within(layer + 1, 1, DEPTH - 1,
                                                   skip_runtime_bounds_check_because="the If bounds it")
                    load_tables(following, layer + 2)
                layer_norm(here, 1)

        @block.scalar
        def _(act):
            def split_hi(s, uses):
                act.wait_ge(raw_full[s], (uses + 1) * 16)
                act.activation(w_hi[:, s, :], raw[:, s, :], ACT.Copy).then_inc(hi_ready[s], 1)

            def chunk_done(here, c, turn=0):
                act.wait_ge(w_used[c % SLOTS], here.uses(c, turn) + 1)

            def split_after(here, c, turn=0):
                split_hi(c % SLOTS, here.uses(c, turn) + 1)

            def squares(n, j):
                act.activation(work_of[n][:, 2 * j:2 * j + 2, :], x[:, 2 * j:2 * j + 2, :], ACT.Square
                               ).then_inc(sq_ready.sem, 1)

            def norm_input(here, n, gains, pairs):
                if n in (0, 3):
                    act.wait_ge(gain_ready.sem, here.at(gain_ready, n // 3))
                for j in pairs:
                    act.wait_ge(x_ready.sem, here.at(x_ready, HALVES * (n - 1) + j + 1))
                    for k in (2 * j, 2 * j + 1):
                        act.activation(br_hi[:, k, :], x[:, k, :], ACT.Copy, scale=gains[:, k:k + 1]).then_inc(xg_hi.sem, 1)
                    if n:
                        squares(n, j)

            def norm_mean(here, n):
                act.wait_ge(ss_ready.sem, here.at(ss_ready, n + 1))
                if n == 1:
                    act.activation(floor[:, :], banks[6][:, 0, 0:TT], ACT.Identity, bias=floor0, scale=HEAD_DIM * EPS)
                act.activation(ms[:, :], banks[6][:, 0, 0:TT], ACT.Identity, bias=eps6).then_inc(ms_ready.sem, 1)

            def norm_upper(here, n):
                for k in range(DT):
                    act.wait_ge(xnf_ready.sem, here.at(xnf_ready, DT * n + k + 1))
                    act.activation(in_hi[:, k, :], work_of[n][:, k, :], ACT.Copy).then_inc(xn_hi.sem, 1)

            def hidden_upper(here, n, place=hid_hi):
                act.wait_ge(prod_ready.sem, here.at(prod_ready, n + 1))
                act.activation(place[:, 0:2, :], hidden, ACT.Copy).then_inc(hid_hi_ready.sem, 1)

            def ffn(here, c0, f):
                final = c0 + FFN_CHUNKS - 1

                def step(kind, i, c, turn):
                    if c != final:
                        chunk_done(here, c, turn)
                    if c == c0:
                        norm_mean(here, 2 * f)
                        act.activation(glu_a, banks[4][:, :, :], ACT.Copy).then_inc(gate_out.sem, 1)
                        split_after(here, c, turn)
                        act.wait_ge(gate_scaled.sem, here.at(gate_scaled, 2 * f + 1))
                        act.activation(glu_a, glu_a, ACT.Silu).then_inc(gate_act.sem, 1)
                        norm_upper(here, 2 * f)
                        return
                    if kind == "A":
                        act.activation(glu_a, banks[4][:, :, :], ACT.Silu).then_inc(gate_act.sem, 1)
                    if c == c0 + 1:
                        hidden_upper(here, f * PAIRS)
                    if c == final - 2:
                        hidden_upper(here, f * PAIRS + PAIRS - 1, att_hi)
                    if kind == "D" and c < final - 1:
                        hidden_upper(here, i + (f * PAIRS + 1))
                    if c != final:
                        split_after(here, c, turn)
                ffn_walk(act, c0, step)

            def softmax_exp(here, h, keys, scale):
                act.wait_ge(nmax_ready.sem, here.at(nmax_ready, h + 1))
                b = h % 2
                for a in range(TT):
                    part = soft[:, b, a, 0:keys[a]]
                    e = act.activation(part, part, ACT.Exp, bias=stat[:, b, 2 + a:3 + a], scale=scale(a),
                                       accum_out=stat[:, b, 4 + a:5 + a])
                e.then_inc(exp_ready.sem, 1)

            def turn_halves(here, n, two):
                half, place = TURN[here.kind], turned_places[here.kind][n % 2]
                if n >= 2:
                    act.wait_ge(qk_ready.sem, here.at(qk_ready, n - 1))
                for at in range(0, P, half):
                    other = at + half if at // half % 2 == 0 else at - half
                    act.dma_start(place[at:at + half], two[other:other + half]).then_inc(qk_turned[n % 2].sem, 16)

            def weights_out(here, h, keys):
                act.wait_ge(p_turned.sem, here.at(p_turned, h + 1))
                if h >= 2:
                    act.wait_ge(pv_done.sem, here.at(pv_done, h - 1))
                n = sum(keys)
                act.activation(flat(softT[:, h % 2, :, :])[:, 0:n], flat(banks[6][:, :, :])[:, 0:n], ACT.Copy
                               ).then_inc(pT_ready.sem, 1)

            def attention_out(here, j):
                act.wait_ge(pv_done.sem, here.at(pv_done, 2 * j + 2))
                act.activation(att_hi[:, j, :], banks[7][:, j % 2, :], ACT.Copy).then_inc(att_hi_ready.sem, 1)

            def merged_upper(here, merged, upper, j):
                act.wait_ge(merged_ready.sem, here.at(merged_ready, j + 1))
                act.activation(upper[:, 2 * j:2 * j + 2, :], merged[:, 2 * j:2 * j + 2, :], ACT.Copy
                               ).then_inc(merged_hi.sem, 1)

            norm_input(Place(0, 0), 0, gain1, range(HALVES))
            split_hi(0, 0)
            for j in range(HALVES):
                squares(0, j)
            split_hi(1, 0)
            act.wait_ge(small_set, SMALL)

            with act.Fori(0, DEPTH) as layer:
                here = Place(0, layer)
                split_hi(2, here.uses(2))
                ffn(here, 0, 0)
                norm_input(here, 1, cur[:, C_MIX:C_MIX + DT], range(HALVES))
                split_hi(2, here.uses(FFN_CHUNKS + 2))
                for m in range(MIX1):
                    c = FFN_CHUNKS + m
                    chunk_done(here, c)
                    bank = banks[4 + m % 2]
                    if m == 0:
                        norm_mean(here, 1)
                    if m < 4:
                        col = C_Q if m < 2 else C_K
                        act.activation(qk[:, 2 * m:2 * m + 2, :], bank[:, :, :], ACT.Copy, scale=cur[:, col:col + 1]
                                       ).then_inc(mix_evac.sem, 1)
                        if m >= 2:
                            act.wait_ge(qk_ms.sem, here.at(qk_ms, m - 1))
                        act.activation(qk_sq[:, m % 2, :], flat(bank[:, :, :]), ACT.Square).then_inc(qk_sq_ready.sem, 1)
                    elif m < 6:
                        act.activation(v_tok[:, :, (m - 4) * T:(m - 3) * T], bank[:, :, :], ACT.Copy
                                       ).then_inc(mix_evac.sem, 1)
                    elif m < 8:
                        act.activation(u[:, 2 * (m - 6):2 * (m - 5), :], bank[:, :, :], ACT.Copy).then_inc(mix_evac.sem, 1)
                    elif m < 16:
                        branch, j = (m - 8) // HALVES, (m - 8) % HALVES
                        for a in range(2):
                            f = 2 * j + a
                            col = C_GATE + DT * branch + f
                            e = act.activation(gates1[branch][:, f, :], bank[:, a, :], ACT.Identity, bias=cur[:, col:col + 1])
                        e.then_inc(mix_evac.sem, 1)
                    if m in (1, 2, 4, 5):
                        p = m - 1 if m < 3 else m - 2
                        act.wait_ge(mix_evac.sem, here.at(mix_evac, p + 1))
                        turn_halves(here, p, qk[:, 2 * p:2 * p + 2, :])
                    if m == 0:
                        split_after(here, c)
                        norm_upper(here, 1)
                    if 1 <= m < 5:
                        p = m - 1
                        act.wait_ge(qk_ms.sem, here.at(qk_ms, m))
                        for a in range(TT):
                            at = a * 2 * HEADS + 4 * p
                            least, scale = (floor[:, a:a + 1], float(HEAD_DIM)) if p < 2 else (eps6, 1.0)
                            e = act.activation(qk_var[:, a, 4 * p:4 * p + 4], banks[0][:, 0, at:at + 4], ACT.Identity,
                                               bias=least, scale=scale)
                        e.then_inc(qk_var_ready.sem, 1)
                    if m == 10:
                        act.wait_ge(pool_y.sem, here.at(pool_y, 1))
                        for g in range(4):
                            act.activation(br_hi[:, g, :], banks[g // 2][:, g % 2, :], ACT.Copy,
                                           scale=cur[:, C_SCALE + g:C_SCALE + g + 1]).then_inc(pool_hi.sem, 1)
                    if 0 <= m - 8 < HEADS:
                        weights_out(here, m - 8, CAUSAL_KEYS)
                    if m >= 10 and m % 2 == 0 and (m - 10) // 2 < HALVES:
                        attention_out(here, (m - 10) // 2)
                    if 0 <= m - 7 < HEADS:
                        softmax_exp(here, m - 7, CAUSAL_KEYS, lambda a: qk_rs[:, a, m - 7:m - 6])
                    if m == 18:
                        for j in range(HALVES):
                            merged_upper(here, merged1, in_hi, j)
                            if j == 1:
                                split_after(here, c)
                    if m >= 20:
                        norm_input(here, 2, cur[:, C_FFN2:C_FFN2 + DT], [m - 20])
                    if 0 < m < MIX1 - 1 and m != 18:
                        split_after(here, c)
                    if m in (15, 16):
                        gates = gates1[m - 15]
                        act.wait_ge(mix_evac.sem, here.at(mix_evac, 12 + 4 * (m - 15)))
                        act.activation(gates[:, :, :], gates[:, :, :], ACT.Sigmoid).then_inc(sig_ready.sem, 1)
                    if m in (3, 4):
                        p = m - 1
                        act.wait_ge(qk_rs_ready.sem, here.at(qk_rs_ready, p + 1))
                        if m == 4:
                            act.wait_ge(k_spread.sem, here.at(k_spread, 1))
                        act.activation(k_cols[:, :, :].rearrange("p a (h d) -> p a h d", d=HEAD_DIM),
                                       qk_rs[:, :, 4 * p:4 * p + 4].unsqueeze(3).broadcast_to([P, TT, 4, HEAD_DIM]), ACT.Copy
                                       ).then_inc(k_cols_ready.sem, 1)
                split_hi(2, here.uses(FFN_CHUNKS + MIX1 + 2))
                ffn(here, FFN_CHUNKS + MIX1, 1)
                norm_input(here, 3, gain1, range(HALVES))

            act.wait_ge(col2_in, 16)
            last = col2[:, :, C_LF:COLS2]
            steps = [decay[:, n, :].rearrange("p (l c) -> p l c", l=DEPTH) for n in range(4)]
            act.activation(steps[0], last, ACT.Abs).then_inc(decay_scal, 1)
            act.wait_ge(decay_scal, 1)
            act.activation(steps[1], steps[0], ACT.Exp, scale=-1.0).then_inc(decay_scal, 1)
            act.wait_ge(decay_scal, 2)
            act.activation(steps[2], steps[1], ACT.Ln, bias=1.0).then_inc(decay_scal, 1)

            with act.Fori(0, DEPTH) as layer:
                here = Place(1, layer)
                act.wait_ge(xs_ready.sem, here.at(xs_ready, 0))
                split_hi(2, here.uses(2))

                def layer_norm(n, col_b, spare=lambda: None):
                    act.wait_ge(var_ready.sem, here.at(var_ready, n + 1))
                    act.activation(ms[:, :], banks[7][:, 0, 0:TT], ACT.Identity, bias=eps5).then_inc(ln_var.sem, 1)
                    spare()
                    for k in range(DT):
                        act.wait_ge(ln_scaled.sem, here.at(ln_scaled, DT * n + k + 1))
                        act.activation(x[:, k, :], work[:, k, :], ACT.Identity, bias=cur[:, col_b + k:col_b + k + 1]
                                       ).then_inc(x_new.sem, 1)
                        act.activation(br_hi[:, k, :], work[:, k, :], ACT.Identity,
                                       bias=cur[:, col_b + k:col_b + k + 1]).then_inc(xs_hi.sem, 1)

                def centred_squares(n):
                    for k in range(DT):
                        act.wait_ge(c_ready.sem, here.at(c_ready, DT * n + k + 1))
                        act.activation(work[:, k, :], x[:, k, :], ACT.Square).then_inc(c_sq.sem, 1)

                for m in range(MIX2):
                    chunk_done(here, m)
                    bank = banks[4 + m % 2]
                    if m < 4:
                        act.activation(qk[:, 2 * m:2 * m + 2, :], bank[:, :, :], ACT.Copy,
                                       scale=HEAD_DIM ** -0.5 if m < 2 else 1.0).then_inc(mix_evac.sem, 1)
                    elif m < 6:
                        act.activation(v_tok[:, :, (m - 4) * T:(m - 3) * T], bank[:, :, :], ACT.Copy
                                       ).then_inc(mix_evac.sem, 1)
                    elif m < 10:
                        two = ret_qk[:, 2 * (m - 6):2 * (m - 5), :]
                        act.activation(two, bank[:, :, :], ACT.Copy).then_inc(mix_evac.sem, 1)
                        if m == 6:
                            act.wait_ge(dist_ready.sem, here.at(dist_ready, RET_HEADS))
                        act.wait_ge(mix_evac.sem, here.at(mix_evac, m + 1))
                        turn_halves(here, m - 6, two)
                    elif m < 14:
                        if m == 13:
                            act.wait_ge(qk_ready.sem, here.at(qk_ready, 4))
                        act.activation(ret_v[:, :, (m - 10) * T:(m - 9) * T], bank[:, :, :], ACT.Copy
                                       ).then_inc(mix_evac.sem, 1)
                    elif m < 18:
                        if m == 14:
                            act.wait_ge(max_ready.sem, here.at(max_ready, HEADS))
                        act.activation(silu_g[:, 2 * (m - 14):2 * (m - 13), :], bank[:, :, :], ACT.Silu
                                       ).then_inc(mix_evac.sem, 1)
                    elif m < 22 or 24 <= m < 28:
                        j = m - 18 if m < 22 else m - 24
                        if m == 24:
                            act.wait_ge(branch_evac.sem, here.at(branch_evac, 2))
                        act.activation(gates2[:, 2 * j:2 * j + 2, :], bank[:, :, :], ACT.Sigmoid).then_inc(mix_evac.sem, 1)
                    elif m >= 38:
                        j = m - 38
                        if m >= 40:
                            act.wait_ge(ple_mul.sem, here.at(ple_mul, j - 1))
                        act.activation(ple_gate[:, j % 2, :], flat(bank[:, :, :]), ACT.Sigmoid).then_inc(mix_evac.sem, 1)
                    if 4 <= m < 4 + RET_HEADS:
                        h = m - 4
                        act.wait_ge(dist_ready.sem, here.at(dist_ready, h + 1))
                        act.activation(decays[:, h, :], decays[:, h, :], ACT.Exp).then_inc(decay_ready.sem, 1)
                    if 0 <= m - 6 < HEADS:
                        weights_out(here, m - 6, ALL_KEYS)
                    if m >= 8 and m % 2 == 0 and (m - 8) // 2 < HALVES:
                        attention_out(here, (m - 8) // 2)
                    if 0 <= m - 5 < HEADS:
                        softmax_exp(here, m - 5, ALL_KEYS, lambda a: 1.0)
                    if 0 <= m - 18 < RET_HEADS:
                        h = m - 18
                        split_after(here, m)
                        act.wait_ge(ret_y.sem, here.at(ret_y, h + 1))
                        act.activation(in_hi[:, 2 * h:2 * h + 2, :], silu_g[:, 2 * h:2 * h + 2, :], ACT.Copy
                                       ).then_inc(ret_hi.sem, 1)
                    if m == 24:
                        act.wait_ge(ple_in_sem, (layer + 1) * 16)
                        act.activation(ple_hi[:, :, :], ple_in[:, :, :], ACT.Copy).then_inc(ple_split_hi.sem, 1)
                    if 28 <= m < 31:
                        split_after(here, m)
                        merged_upper(here, merged2, br_hi, m - 28)
                    elif m == 31:
                        merged_upper(here, merged2, br_hi, m - 28)
                        split_after(here, m)
                    elif m == 35:
                        split_after(here, m)
                        centred_squares(0)
                    elif m == 36:
                        def ple_first():
                            for a in range(2):
                                e = act.activation(ple_out[:, 2 * a:2 * a + 2, :], banks[4 + a][:, :, :], ACT.Copy)
                            e.then_inc(mix_evac.sem, 1)
                            split_after(here, m)
                        layer_norm(0, C_B1, ple_first)
                    elif m == 37:
                        for a in range(2):
                            e = act.activation(ple_out[:, 4 + 2 * a:6 + 2 * a, :], banks[2 + a][:, :, :], ACT.Copy)
                        e.then_inc(mix_evac.sem, 1)
                        split_after(here, m)
                    elif not 0 <= m - 18 < RET_HEADS:
                        split_after(here, m)

                def step(kind, i, c, turn):
                    final = c == CHUNKS[1] - 1
                    if c < CHUNKS[1] - 2:
                        chunk_done(here, c, turn)
                    if kind == "A":
                        for a in range(2):
                            mid = cur[:, bass.ds(i * 2 + (C_TAP + FT + a), 1)]
                            add = cur[:, bass.ds(i * 2 + (C_CONVB + a), 1)]
                            e = act.activation(glu_a[:, a, :], banks[4][:, a, :], ACT.Identity, bias=add, scale=mid)
                        e.then_inc(gate_act.sem, 1)
                    if kind == "B":
                        for a in range(2):
                            mid = cur[:, bass.ds(i * 2 + (C_TAP + FT + FT // 2 + a), 1)]
                            add = cur[:, bass.ds(i * 2 + (C_CONVB + FT // 2 + a), 1)]
                            e = act.activation(glu_b[:, a, :], banks[5][:, a, :], ACT.Identity, bias=add, scale=mid)
                        e.then_inc(up_mid.sem, 1)
                        act.wait_ge(gate_taps.sem, here.at(gate_taps, i + 1))
                        act.activation(glu_a, glu_a, ACT.Gelu_apprx_tanh).then_inc(gelu_ready.sem, 1)
                        if c == MIX2 + 1:
                            hidden_upper(here, 0)
                        if c == CHUNKS[1] - 3:
                            hidden_upper(here, PAIRS - 1, att_hi)
                    if kind == "D" and c < CHUNKS[1] - 2:
                        hidden_upper(here, i + 1)
                    if c in (CHUNKS[1] - 3, CHUNKS[1] - 2):
                        with act.If(layer < DEPTH - 1):
                            if c == CHUNKS[1] - 2:
                                chunk_done(here, c, turn)
                            split_after(here, c, turn)
                    elif not final:
                        split_after(here, c, turn)
                ffn_walk(act, MIX2, step)
                centred_squares(1)
                layer_norm(1, C_B2)

        @block.vector
        def _(dve):
            def split_lo(s, uses):
                dve.wait_ge(hi_ready[s], uses + 1)
                dve.tensor_tensor(w_lo[:, s, :], raw[:, s, :], w_hi[:, s, :].bitcast(F32), ALU.subtract
                                  ).then_inc(lo_ready[s], 1)

            def chunk_done(here, c, turn=0):
                dve.wait_ge(w_used[c % SLOTS], here.uses(c, turn) + 1)

            def split_after(here, c, turn=0):
                split_lo(c % SLOTS, here.uses(c, turn) + 1)

            def rest(out, whole, upper):
                return dve.tensor_tensor(out, whole, upper.bitcast(F32), ALU.subtract)

            def xg_lower(here, n, gains, pairs):
                for k in range(2 * pairs[0], 2 * pairs[-1] + 2):
                    dve.wait_ge(xg_hi.sem, here.at(xg_hi, DT * (n - 1) + k + 1))
                    dve.scalar_tensor_tensor(out=br_lo[:, k, :], in0=x[:, k, :], scalar=gains[:, k:k + 1],
                                             in1=br_hi[:, k, :].bitcast(F32), op0=ALU.mult, op1=ALU.subtract
                                             ).then_inc(xg_ready.sem, 1)

            def norm_factor(here, n):
                dve.wait_ge(rstd_ready.sem, here.at(rstd_ready, n + 1))

            def norm(here, n, gains):
                for k in range(DT):
                    dve.scalar_tensor_tensor(out=work_of[n][:, k, :], in0=x[:, k, :], scalar=gains[:, k:k + 1],
                                             in1=rstd_norm, op0=ALU.mult, op1=ALU.mult).then_inc(xnf_ready.sem, 1)

            def hidden_lower(here, n, upper=hid_hi, place=hid_lo):
                dve.wait_ge(hid_hi_ready.sem, here.at(hid_hi_ready, n + 1))
                rest(place[:, 0:2, :], hidden, upper[:, 0:2, :]).then_inc(hid_ready.sem, 1)

            def ffn(here, c0, f, gains, n_next, next_gains):
                final = c0 + FFN_CHUNKS - 1

                def step(kind, i, c, turn):
                    if c != final:
                        chunk_done(here, c, turn)
                    if c == c0:
                        factor = rstd_norm.unsqueeze(1).broadcast_to([P, 2, T])
                        norm_factor(here, 2 * f)
                        dve.wait_ge(gate_out.sem, here.at(gate_out, f + 1))
                        dve.tensor_tensor(glu_a, glu_a, factor, ALU.mult).then_inc(gate_scaled.sem, 1)
                        norm(here, 2 * f, gains)
                        dve.wait_ge(gate_act.sem, here.at(gate_act, f * PAIRS + 1))
                        dve.tensor_tensor(glu_a, glu_a, factor, ALU.mult).then_inc(gate_scaled.sem, 1)
                        split_after(here, c, turn)
                        return
                    if kind == "B":
                        if c == c0 + 1:
                            dve.wait_ge(gate_scaled.sem, here.at(gate_scaled, 2 * f + 2))
                        else:
                            dve.wait_ge(gate_act.sem, here.at(gate_act, i + (f * PAIRS + 1)))
                            dve.wait_ge(hid_ready.sem, here.at(hid_ready, i + f * PAIRS))
                        dve.tensor_tensor(hidden, glu_a, banks[5][:, :, :], ALU.mult).then_inc(prod_ready.sem, 1)
                    if c == c0 + 1:
                        hidden_lower(here, f * PAIRS)
                    if c == final - 2:
                        hidden_lower(here, f * PAIRS + PAIRS - 1, att_hi, att_lo)
                    if kind == "D" and c < final - 1:
                        hidden_lower(here, i + (f * PAIRS + 1))
                    if c < final - 1:
                        split_after(here, c, turn)
                    elif c == final:
                        for j in range(HALVES):
                            if j < HALVES - 1:
                                dve.wait_ge(acc_done.sem, here.at(acc_done, f * (HALVES - 1) + j + 1))
                            else:
                                chunk_done(here, c)
                            two = x[:, 2 * j:2 * j + 2, :]
                            dve.scalar_tensor_tensor(out=two, in0=banks[j][:, :, :], scalar=0.5, in1=two, op0=ALU.mult,
                                                     op1=ALU.add).then_inc(x_ready.sem, 1)
                            if j >= 1:
                                xg_lower(here, n_next, next_gains, [j - 1])
                        xg_lower(here, n_next, next_gains, [HALVES - 1])
                        split_after(here, c - 1)
                ffn_walk(dve, c0, step)

            def softmax_scores(here, h, keys, added, scale=None):
                b = h % 2
                dve.wait_ge(scored.sem, here.at(scored, h + 1))
                if h >= 2:
                    dve.wait_ge(p_turned.sem, here.at(p_turned, h - 1))
                dve.memset(stat[:, b, 4:6], 0.0)
                for a in range(TT):
                    e = dve.tensor_tensor_reduce(soft[:, b, a, 0:keys[a]], banks[2 + b][:, a, 0:keys[a]], added(a), 1.0, LOWEST,
                                                 ALU.add, ALU.max, stat[:, b, a:a + 1])
                e.then_inc(max_ready.sem, 1)
                dve.wait_ge(max_ready.sem, here.at(max_ready, h + 1))
                low, top = stat[:, b, 2:4], stat[:, b, 0:2]
                if scale is None:
                    e = dve.tensor_scalar(low, top, -1.0, None, ALU.mult)
                else:
                    e = dve.scalar_tensor_tensor(out=low, in0=top, scalar=-1.0, in1=scale, op0=ALU.mult, op1=ALU.mult)
                e.then_inc(nmax_ready.sem, 1)

            def softmax_weights(here, h):
                b = h % 2
                dve.wait_ge(exp_ready.sem, here.at(exp_ready, h + 1))
                dve.reciprocal(stat[:, b, 6:8], stat[:, b, 4:6]).then_inc(inv_ready.sem, 1)
                dve.wait_ge(inv_ready.sem, here.at(inv_ready, h + 1))
                if h >= 1:
                    dve.wait_ge(p_turned.sem, here.at(p_turned, h))
                dve.tensor_tensor(weigh[:, :, :], ident.unsqueeze(1).broadcast_to([P, TT, P]),
                                  stat[:, b, 6:8].unsqueeze(2).broadcast_to([P, TT, P]), ALU.mult
                                  ).then_inc(weigh_ready.sem, 1)

            def attention_lower(here, j):
                dve.wait_ge(att_hi_ready.sem, here.at(att_hi_ready, j + 1))
                rest(att_lo[:, j, :], banks[7][:, j % 2, :], att_hi[:, j, :]).then_inc(att_ready.sem, 1)

            def turn_pairs(here, n, two, cos, sin):
                turned = turned_places[here.kind][n % 2]
                arrived = qk_turned[n % 2]
                dve.wait_ge(arrived.sem, here.at(arrived, (n // 2 + 1) * 16 * P // TURN[here.kind]))
                dve.tensor_tensor(turned, turned, table(sin), ALU.mult).then_inc(qk_sin.sem, 1)
                dve.tensor_tensor(two, two, table(cos), ALU.mult).then_inc(qk_cos.sem, 1)
                dve.wait_ge(qk_sin.sem, here.at(qk_sin, n + 1))
                dve.wait_ge(qk_cos.sem, here.at(qk_cos, n + 1))
                dve.tensor_tensor(two, two, turned, ALU.add).then_inc(qk_ready.sem, 1)

            dve.sem_inc(xs_hi.sem, DT)
            dve.sem_inc(xs_ready.sem, DT)

            def next_gains(l):
                dve.tensor_copy(gain1[:, :], col1[:, bass.ds(l, 1), C_FFN1:C_FFN1 + DT].rearrange("p a c -> p (a c)")
                                ).then_inc(gain_ready.sem, 1)

            dve.wait_ge(col1_in, 16)
            next_gains(0)
            dve.wait_ge(gain_ready.sem, 1)
            for j in range(HALVES):
                dve.wait_ge(x_in[j], 16)
                dve.sem_inc(x_ready.sem, 1)
                xg_lower(Place(0, 0), 0, gain1, [j])
            for s in range(2):
                split_lo(s, 0)

            with dve.Fori(0, DEPTH) as layer:
                here = Place(0, layer)
                dve.tensor_copy(cur[:, 0:COLS1], col1[:, bass.ds(layer, 1), :].rearrange("p a c -> p (a c)")
                                ).then_inc(cur_ready.sem, 1)
                dve.wait_ge(cur_ready.sem, here.at(cur_ready, 1))
                split_lo(2, here.uses(2))
                ffn(here, 0, 0, gain1, 1, cur[:, C_MIX:C_MIX + DT])
                next_gains(layer + 1)
                dve.wait_ge(gain_ready.sem, here.at(gain_ready, 1))
                split_lo(2, here.uses(FFN_CHUNKS + 2))
                for m in range(MIX1):
                    c = FFN_CHUNKS + m
                    chunk_done(here, c)
                    if m == 0:
                        norm_factor(here, 1)
                        norm(here, 1, cur[:, C_MIX:C_MIX + DT])
                        split_after(here, c)
                    if 0 <= m - 7 < HEADS:
                        softmax_scores(here, m - 7, CAUSAL_KEYS, lambda a: causal[:, a, 0:CAUSAL_KEYS[a]],
                                       qk_rs[:, :, m - 7])
                    if m == 3:
                        dve.wait_ge(konst_in, 16)
                    if 3 <= m < 7:
                        p = m - 3
                        two = qk[:, 2 * p:2 * p + 2, :]
                        turn_pairs(here, p, two, K_COS1, K_SIN1)
                        if p >= 2:
                            dve.wait_ge(qk_ready.sem, here.at(qk_ready, p + 1))
                            dve.wait_ge(k_spread.sem, here.at(k_spread, p - 1))
                            dve.tensor_tensor(two, two, banks[p][:, :, :], ALU.mult).then_inc(k_normed.sem, 1)
                    if m == 10:
                        dve.wait_ge(pool_hi.sem, here.at(pool_hi, 4))
                        for g in range(4):
                            e = dve.scalar_tensor_tensor(out=br_lo[:, g, :], in0=banks[g // 2][:, g % 2, :],
                                                         scalar=cur[:, C_SCALE + g:C_SCALE + g + 1],
                                                         in1=br_hi[:, g, :].bitcast(F32), op0=ALU.mult, op1=ALU.subtract)
                        e.then_inc(pool_ready.sem, 1)
                    if m in (16, 17):
                        if m == 16:
                            dve.wait_ge(sig_ready.sem, here.at(sig_ready, 1))
                        for a in range(2):
                            f = 4 * (m - 16) + 2 * a
                            part = merged1[:, f:f + 2, :]
                            e = dve.tensor_tensor(part, part, banks[f // 2][:, :, :], ALU.mult)
                        e.then_inc(branch_evac.sem, 1)
                    if m >= 10 and m % 2 == 0 and (m - 10) // 2 < HALVES:
                        attention_lower(here, (m - 10) // 2)
                    if 0 <= m - 7 < HEADS:
                        softmax_weights(here, m - 7)
                    if m == 18:
                        dve.wait_ge(sig_ready.sem, here.at(sig_ready, 2))
                        dve.wait_ge(branch_evac.sem, here.at(branch_evac, 2))
                        for j in range(HALVES):
                            f = 2 * j
                            if j == 2:
                                dve.wait_ge(attn_pair.sem, here.at(attn_pair, 1))
                            elif j == 3:
                                chunk_done(here, c + 1)
                            part = gates1[1][:, f:f + 2, :]
                            dve.tensor_tensor(part, part, banks[(4, 5, 2, 3)[j]][:, :, :], ALU.mult
                                              ).then_inc(part_ready.sem, 1)
                            dve.wait_ge(part_ready.sem, here.at(part_ready, j + 1))
                            dve.tensor_tensor(merged1[:, f:f + 2, :], merged1[:, f:f + 2, :], part, ALU.add
                                              ).then_inc(merged_ready.sem, 1)
                    if m >= 20:
                        j = m - 20
                        two = x[:, 2 * j:2 * j + 2, :]
                        dve.tensor_tensor(two, two, banks[j][:, :, :], ALU.add).then_inc(x_ready.sem, 1)
                        if j >= 1:
                            xg_lower(here, 2, cur[:, C_FFN2:C_FFN2 + DT], [j - 1])
                    if 0 < m < MIX1 - 2:
                        split_after(here, c)
                xg_lower(here, 2, cur[:, C_FFN2:C_FFN2 + DT], [HALVES - 1])
                split_after(here, FFN_CHUNKS + MIX1 - 2)
                split_lo(2, here.uses(FFN_CHUNKS + MIX1 + 2))
                ffn(here, FFN_CHUNKS + MIX1, 1, cur[:, C_FFN2:C_FFN2 + DT], 3, gain1)

            steps = [decay[:, n, :].rearrange("p (l c) -> p l c", l=DEPTH) for n in range(4)]
            last = col2[:, :, C_LF:COLS2]
            dve.wait_ge(decay_scal, 3)
            dve.tensor_scalar(steps[3], last, 0.0, None, ALU.min).then_inc(decay_step, 1)
            dve.wait_ge(decay_step, 1)
            dve.tensor_tensor(last[:, :, 0:RET_HEADS], steps[3][:, :, 0:RET_HEADS], steps[2][:, :, 0:RET_HEADS],
                              ALU.subtract).then_inc(decay_step, 1)
            dve.tensor_tensor(last[:, :, RET_HEADS:], steps[2][:, :, RET_HEADS:], steps[3][:, :, RET_HEADS:],
                              ALU.subtract).then_inc(decay_step, 1)
            dve.wait_ge(decay_step, 3)

            with dve.Fori(0, DEPTH) as layer:
                here = Place(1, layer)
                dve.wait_ge(xs_hi.sem, here.at(xs_hi, 0))
                dve.tensor_copy(cur[:, 0:COLS2], col2[:, bass.ds(layer, 1), :].rearrange("p a c -> p (a c)")
                                ).then_inc(cur_ready.sem, 1)
                dve.wait_ge(cur_ready.sem, here.at(cur_ready, 1))
                split_lo(2, here.uses(2))

                def centred(n):
                    dve.wait_ge(mu_ready.sem, here.at(mu_ready, n + 1))
                    for k in range(DT):
                        dve.tensor_tensor(x[:, k, :], x[:, k, :], banks[6][:, 0, :], ALU.subtract).then_inc(c_ready.sem, 1)

                def layer_norm(n, col):
                    dve.wait_ge(ln_rstd.sem, here.at(ln_rstd, n + 1))
                    for k in range(DT):
                        dve.scalar_tensor_tensor(out=work[:, k, :], in0=x[:, k, :], scalar=cur[:, col + k:col + k + 1],
                                                 in1=rstd_ln, op0=ALU.mult, op1=ALU.mult).then_inc(ln_scaled.sem, 1)

                for m in range(MIX2):
                    chunk_done(here, m)
                    if 0 <= m - 5 < HEADS:
                        def near(a, h=m - 5):
                            r = (h * ROW_STEPS + (TT - 1 - a) * (P // GRID_W)) * GRID_W
                            return area4[:, r:r + T]
                        if m == 5:
                            dve.wait_ge(bias_ready.sem, here.at(bias_ready, 1))
                        softmax_scores(here, m - 5, ALL_KEYS, near)
                    if 7 <= m < 11:
                        turn_pairs(here, m - 7, ret_qk[:, 2 * (m - 7):2 * (m - 6), :], K_COS2, K_SIN2)
                    if 0 <= m - 15 < RET_HEADS:
                        h = m - 15
                        dve.wait_ge(ret_scored.sem, here.at(ret_scored, h + 1))
                        dve.wait_ge(decay_ready.sem, here.at(decay_ready, h + 1))
                        if h >= 2:
                            dve.wait_ge(ret_pv.sem, here.at(ret_pv, h - 1))
                        dve.scalar_tensor_tensor(out=flat(softT[:, h % 2, :, :]), in0=flat(banks[2 + h % 2][:, :, :]),
                                                 scalar=RET_QK ** -0.5, in1=decays[:, h, :], op0=ALU.mult, op1=ALU.mult
                                                 ).then_inc(ret_p.sem, 1)
                    if 0 <= m - 18 < RET_HEADS:
                        h = m - 18
                        dve.wait_ge(ret_turned.sem, here.at(ret_turned, h + 1))
                        gated = silu_g[:, 2 * h:2 * h + 2, :]
                        dve.tensor_tensor(gated, gated, banks[6][:, :, :], ALU.mult).then_inc(ret_y.sem, 1)
                    if 0 <= m - 16 < RET_HEADS:
                        h = m - 16
                        b = h % 2
                        dve.wait_ge(ret_pv.sem, here.at(ret_pv, h + 1))
                        for a in range(TT):
                            e = dve.bn_stats(group[:, b, a, 0:6], banks[b][:, a, :])
                        e.then_inc(ret_stats.sem, 1)
                        dve.wait_ge(ret_stats.sem, here.at(ret_stats, h + 1))
                        dve.memset(group[:, b, :, 8:9], GN_EPS)
                        for a in range(TT):
                            e = dve.bn_aggr(group[:, b, a, 6:8], group[:, b, a, 0:6])
                        e.then_inc(ret_mv.sem, 1)
                        dve.wait_ge(ret_mv.sem, here.at(ret_mv, h + 1))
                        dve.tensor_tensor(group[:, b, :, 10:11], group[:, b, :, 7:8], group[:, b, :, 8:9], ALU.add
                                          ).then_inc(ret_var.sem, 1)
                        split_after(here, m)
                        dve.wait_ge(ret_rstd.sem, here.at(ret_rstd, h + 1))
                        for a in range(TT):
                            e = dve.tensor_scalar(soft[:, b, a, :], banks[b][:, a, :], group[:, b, a, 6:7],
                                                  group[:, b, a, 11:12], ALU.subtract, ALU.mult)
                        e.then_inc(ret_o.sem, 1)
                    if m in (22, 23):
                        for a in range(2):
                            f = 4 * (m - 22) + 2 * a
                            if a == 0:
                                dve.wait_ge(mix_evac.sem, here.at(mix_evac, 22))
                            e = dve.tensor_tensor(merged2[:, f:f + 2, :], gates2[:, f:f + 2, :],
                                                  banks[2 * (m - 22) + a][:, :, :], ALU.mult)
                        e.then_inc(branch_evac.sem, 1)
                    if 28 <= m < 32:
                        j = m - 28
                        f = 2 * j
                        part = gates2[:, f:f + 2, :]
                        dve.wait_ge(mix_evac.sem, here.at(mix_evac, 26))
                        dve.tensor_tensor(part, part, banks[j % 2][:, :, :], ALU.mult).then_inc(branch_evac.sem, 1)
                        dve.wait_ge(branch_evac.sem, here.at(branch_evac, 3 + j))
                        dve.tensor_tensor(merged2[:, f:f + 2, :], merged2[:, f:f + 2, :], part, ALU.add
                                          ).then_inc(merged_ready.sem, 1)
                    if 32 <= m < 36:
                        two = x[:, 2 * (m - 32):2 * (m - 31), :]
                        dve.scalar_tensor_tensor(out=two, in0=two, scalar=ALPHA, in1=banks[m - 32][:, :, :], op0=ALU.mult,
                                                 op1=ALU.add).then_inc(z_ready.sem, 1)
                    if m >= 38:
                        j = m - 38
                        two = ple_out[:, 2 * j:2 * j + 2, :]
                        dve.wait_ge(mix_evac.sem, here.at(mix_evac, 29 + j))
                        dve.tensor_tensor(flat(two), flat(two), ple_gate[:, j % 2, :], ALU.mult).then_inc(ple_mul.sem, 1)
                        dve.wait_ge(ple_mul.sem, here.at(ple_mul, j + 1))
                        dve.scalar_tensor_tensor(out=x[:, 2 * j:2 * j + 2, :], in0=x[:, 2 * j:2 * j + 2, :], scalar=ALPHA,
                                                 in1=two, op0=ALU.mult, op1=ALU.add).then_inc(base_ready.sem, 1)
                    if m >= 8 and m % 2 == 0 and (m - 8) // 2 < HALVES:
                        attention_lower(here, (m - 8) // 2)
                    if 0 <= m - 5 < HEADS:
                        softmax_weights(here, m - 5)
                    if m == 35:
                        centred(0)
                        split_after(here, m)
                    elif m == 36:
                        layer_norm(0, C_G1)
                        split_after(here, m)
                    elif not 0 <= m - 16 < RET_HEADS:
                        split_after(here, m)

                def taps(out, bank, i, first, left, done, n):
                    for a in range(2):
                        w = cur[:, bass.ds(i * 2 + (first + a), 1)]
                        e = dve.scalar_tensor_tensor(out=out[:, a, 1:T], in0=bank[:, a, 0:T - 1], scalar=w,
                                                     in1=out[:, a, 1:T], op0=ALU.mult, op1=ALU.add)
                    e.then_inc(left.sem, 1)
                    dve.wait_ge(left.sem, here.at(left, n))
                    for a in range(2):
                        w = cur[:, bass.ds(i * 2 + (first + 2 * FT + a), 1)]
                        e = dve.scalar_tensor_tensor(out=out[:, a, 0:T - 1], in0=bank[:, a, 1:T], scalar=w,
                                                     in1=out[:, a, 0:T - 1], op0=ALU.mult, op1=ALU.add)
                    e.then_inc(done.sem, 1)

                def step(kind, i, c, turn):
                    final = c == CHUNKS[1] - 1
                    if c < CHUNKS[1] - 2:
                        chunk_done(here, c, turn)
                    if kind == "A":
                        dve.wait_ge(gate_act.sem, here.at(gate_act, i + 1))
                        taps(glu_a, banks[4], i, C_TAP, gate_left, gate_taps, i + 1)
                    if kind == "B":
                        dve.wait_ge(up_mid.sem, here.at(up_mid, i + 1))
                        taps(glu_b, banks[5], i, C_TAP + FT // 2, up_left, up_taps, i + 1)
                        dve.wait_ge(up_taps.sem, here.at(up_taps, i + 1))
                        dve.wait_ge(gelu_ready.sem, here.at(gelu_ready, i + 1))
                        if c != MIX2 + 1:
                            dve.wait_ge(hid_ready.sem, here.at(hid_ready, i))
                        dve.tensor_tensor(hidden, glu_a, glu_b, ALU.mult).then_inc(prod_ready.sem, 1)
                        if c == MIX2 + 1:
                            hidden_lower(here, 0)
                        if c == CHUNKS[1] - 3:
                            hidden_lower(here, PAIRS - 1, att_hi, att_lo)
                    if kind == "D" and c < CHUNKS[1] - 2:
                        hidden_lower(here, i + 1)
                    if c < CHUNKS[1] - 3:
                        split_after(here, c, turn)
                    elif final:
                        dve.wait_ge(base_ready.sem, here.at(base_ready, 4))
                        for j in range(HALVES):
                            if j < HALVES - 1:
                                dve.wait_ge(acc_done.sem, here.at(acc_done, j + 1))
                            else:
                                chunk_done(here, c)
                            two = x[:, 2 * j:2 * j + 2, :]
                            dve.tensor_tensor(two, two, banks[j][:, :, :], ALU.add).then_inc(z_ready.sem, 1)
                ffn_walk(dve, MIX2, step)
                centred(1)
                with dve.If(layer < DEPTH - 1):
                    chunk_done(here, CHUNKS[1] - 3)
                    split_after(here, CHUNKS[1] - 3)
                layer_norm(1, C_G2)
                with dve.If(layer < DEPTH - 1):
                    chunk_done(here, CHUNKS[1] - 2)
                    split_after(here, CHUNKS[1] - 2)

        @block.tensor
        def _(pe):
            def take(here, c, turn=0):
                pe.wait_ge(lo_ready[c % SLOTS], here.uses(c, turn) + 1)

            def product(out, whi, wlo, xhi, xlo, start, stop):
                pe.matmul(out, whi, xlo, start=start, stop=False, skip_group_check=True)
                pe.matmul(out, wlo, xhi, start=False, stop=False, skip_group_check=True)
                return pe.matmul(out, whi, xhi, start=False, stop=stop, skip_group_check=True)

            def features(c, outs, hi, lo, tiles, k_first=None, fresh=True, stop=True, tile_done=None):
                s, width = c % SLOTS, len(outs) * P

                def one(f, k):
                    at = k * width + f * P
                    return product(outs[f], w_hi[:, s, at:at + P], w_lo[:, s, at:at + P], hi[:, k, :], lo[:, k, :],
                                   start=fresh and k == 0 and f % 2 == 0, stop=stop and k == tiles - 1)

                if k_first is not None:
                    for k in range(tiles):
                        k_first(k)
                        for f in range(len(outs)):
                            e = one(f, k)
                else:
                    for f in range(len(outs)):
                        for k in range(tiles):
                            e = one(f, k)
                        if tile_done and f < len(outs) - 1:
                            tile_done(f, e)
                return e.then_inc(w_used[s], 1)

            def two(bank):
                return [bank[:, a, :] for a in range(2)]

            acc = [banks[f // 2][:, f % 2, :] for f in range(DT)]

            def tokens(c, bank, hi, lo):
                s = c % SLOTS
                for a in range(TT):
                    for k in range(DT):
                        rows, cols = slice(a * P, (a + 1) * P), slice(k * T, (k + 1) * T)
                        e = product(bank[:, a, :], hi[:, k, rows], lo[:, k, rows], w_hi[:, s, cols], w_lo[:, s, cols],
                                    start=a == 0 and k == 0, stop=k == DT - 1)
                return e.then_inc(w_used[s], 1)

            def square_mean(here, n):
                pe.wait_ge(sq_sum.sem, here.at(sq_sum, (HALVES - 1) * (n + 1)))
                for a in range(TT):
                    for f in range(2):
                        e = pe.matmul(banks[6][:, 0, a:a + 1], work_of[n][:, f, a * P:(a + 1) * P], mean_of[:, 0:1],
                                      start=f == 0, stop=f == 1, skip_group_check=True)
                e.then_inc(ss_ready.sem, 1)

            def spread(out, cols):
                for a in range(TT):
                    e = pe.matmul(out[:, a * P:(a + 1) * P], cols(a), ident, start=True, stop=True, skip_group_check=True)
                return e

            def spread_factor(out):
                return spread(out, lambda a: rs[:, a:a + 1].broadcast_to([P, P]))

            def ffn_final(here, c, f):
                s = c % SLOTS
                for t in range(DT):
                    for k in range(2):
                        at = k * D + t * P
                        e = product(acc[t], w_hi[:, s, at:at + P], w_lo[:, s, at:at + P], att_hi[:, k, :],
                                    att_lo[:, k, :], start=False, stop=k == 1)
                    if t % 2:
                        e.then_inc(acc_done.sem if t < DT - 1 else w_used[s], 1)

            def ffn(here, c0, f, start, hi, lo, read_gate, read_up):
                def step(kind, i, c, turn):
                    take(here, c, turn)
                    if kind == "D":
                        pe.wait_ge(hid_ready.sem, here.at(hid_ready, i + (f * PAIRS + 1)))
                        if c == c0 + FFN_CHUNKS - 1:
                            ffn_final(here, c, f)
                        else:
                            features(c, acc, hid_hi, hid_lo, 2, fresh=c == c0 + 4, stop=False)
                    elif not (c0 <= c < c0 + 3 and start(c)):
                        if kind == "A":
                            pe.wait_ge(read_gate.sem, here.at(read_gate, i + f * PAIRS))
                        else:
                            pe.wait_ge(read_up.sem, here.at(read_up, i + f * PAIRS))
                        features(c, two(banks[4 if kind == "A" else 5]), hi, lo, DT)
                ffn_walk(pe, c0, step)

            def scores(here, h, keys, q_ready):
                q_ready()
                rows = slice(HEAD_DIM * (h % 2), HEAD_DIM * (h % 2 + 1))
                for a in range(TT):
                    e = pe.matmul(banks[2 + h % 2][:, a, 0:keys[a]], qk[rows, h // 2, a * P:(a + 1) * P],
                                  qk[rows, HALVES + h // 2, 0:keys[a]], start=True, stop=True, skip_group_check=True)
                e.then_inc(scored.sem, 1)

            def turn_weights(here, h, keys):
                pe.wait_ge(weigh_ready.sem, here.at(weigh_ready, h + 1))
                if h >= 1:
                    pe.wait_ge(pT_ready.sem, here.at(pT_ready, h))
                turned = flat(banks[6][:, :, :])
                at = 0
                for k in range(TT):
                    for a in range(TT):
                        if k * P < keys[a]:
                            e = pe.matmul(turned[:, at:at + P], soft[:, h % 2, a, k * P:(k + 1) * P], weigh[:, a, :],
                                          start=True, stop=True, skip_group_check=True)
                            at += P
                e.then_inc(p_turned.sem, 1)

            def weigh_values(here, h, keys):
                pe.wait_ge(pT_ready.sem, here.at(pT_ready, h + 1))
                j = h // 2
                if j >= 1:
                    pe.wait_ge(att_ready.sem, here.at(att_ready, j))
                rows = slice(HEAD_DIM * (h % 2), HEAD_DIM * (h % 2 + 1))
                weights = flat(softT[:, h % 2, :, :])
                at = 0
                for k in range(TT):
                    n = P * sum(k * P < keys[a] for a in range(TT))
                    e = pe.matmul(banks[7][rows, j % 2, T - n:T], v_tok[:, k, h * HEAD_DIM:(h + 1) * HEAD_DIM],
                                  weights[:, at:at + n], start=k == 0, stop=k == TT - 1, skip_group_check=True)
                    at += n
                e.then_inc(pv_done.sem, 1)

            pe.wait_ge(matrices_in, 16)
            with pe.Fori(0, DEPTH) as layer:
                here = Place(0, layer)

                def normed(n):
                    def wait(k):
                        pe.wait_ge(xn_ready.sem, here.at(xn_ready, DT * n + k + 1))
                    return wait

                def unscaled(n):
                    def wait(k):
                        pe.wait_ge(xg_ready.sem, here.at(xg_ready, DT * (n - 1) + k + 1))
                    return wait

                def norm_start(n, c0):
                    def start(c):
                        if c == c0:
                            features(c, two(banks[4]), br_hi, br_lo, DT, k_first=unscaled(n))
                            square_mean(here, n)
                        elif c == c0 + 1:
                            def factor(k):
                                if k == 3:
                                    pe.wait_ge(rs_ready.sem, here.at(rs_ready, n + 1))
                                    spread_factor(rstd_norm).then_inc(rstd_ready.sem, 1)
                            features(c, two(banks[5]), br_hi, br_lo, DT, k_first=factor)
                        else:
                            if n != 1:
                                pe.wait_ge(gate_out.sem, here.at(gate_out, n // 2 + 1))
                            features(c, two(banks[4]), in_hi, in_lo, DT, k_first=normed(n))
                        return True
                    return start

                ffn(here, 0, 0, norm_start(0, 0), in_hi, in_lo, gate_act, prod_ready)
                def second_half(f, e):
                    if f == 1:
                        e.then_inc(attn_pair.sem, 1)

                for m in range(MIX1):
                    c = FFN_CHUNKS + m
                    bank = banks[4 + m % 2]
                    take(here, c)
                    if 2 <= m < 16:
                        pe.wait_ge(mix_evac.sem, here.at(mix_evac, m - 1))
                    elif m == 16:
                        pe.wait_ge(pool_ready.sem, here.at(pool_ready, 1))
                    elif m == 18:
                        pe.wait_ge(mix_evac.sem, here.at(mix_evac, 16))
                        pe.wait_ge(att_ready.sem, here.at(att_ready, HALVES))
                    elif m == 19:
                        pe.wait_ge(branch_evac.sem, here.at(branch_evac, 2))
                    if m < 3:
                        norm_start(1, FFN_CHUNKS)(c)
                    elif m in (4, 5):
                        tokens(c, bank, in_hi, in_lo)
                    elif 16 <= m < 20:
                        at = (0, 2, 4, 2)[m - 16]
                        outs = two(banks[at]) + two(banks[at + 1])
                        hi, lo = (br_hi, br_lo) if m < 18 else (att_hi, att_lo)
                        features(c, outs, hi, lo, HALVES, tile_done=second_half if m == 19 else None)
                    elif m == 20:
                        features(c, two(banks[m - 20]), in_hi, in_lo, DT, k_first=lambda k: pe.wait_ge(
                            merged_lo.sem, here.at(merged_lo, k // 2 + 1)))
                    elif m > 20:
                        features(c, two(banks[m - 20]), in_hi, in_lo, DT)
                    else:
                        features(c, two(bank), in_hi, in_lo, DT)
                    if 1 <= m < 5:
                        p = m - 1
                        pe.wait_ge(qk_sq_ready.sem, here.at(qk_sq_ready, p + 1))
                        if p >= 1:
                            pe.wait_ge(qk_var_ready.sem, here.at(qk_var_ready, p))
                        for a in range(TT):
                            for f in range(2):
                                at = a * 2 * HEADS + 2 * (2 * p + f)
                                e = pe.matmul(banks[0][:, 0, at:at + 2], qk_sq[:, p % 2, f * T + a * P:f * T + (a + 1) * P],
                                              head_mean, start=True, stop=True, skip_group_check=True)
                        e.then_inc(qk_ms.sem, 1)
                    if m in (4, 5):
                        p = m - 2
                        pe.wait_ge(k_cols_ready.sem, here.at(k_cols_ready, p - 1))
                        for f in range(2):
                            e = spread(banks[p][:, f, :], lambda a: k_cols[:, a, f * P:(f + 1) * P])
                        e.then_inc(k_spread.sem, 1)
                    if m == 10:
                        pe.wait_ge(pool_d.sem, here.at(pool_d, 4))
                        pe.wait_ge(pool_w_ready.sem, here.at(pool_w_ready, 1))
                        for g in range(4):
                            e = pe.matmul(banks[g // 2][:, g % 2, :], pool_cur[:, g * P:(g + 1) * P], sums[g % 2][:, g, :],
                                          start=True, stop=True, skip_group_check=True)
                        e.then_inc(pool_y.sem, 1)
                    if 0 <= m - 7 < HEADS:
                        scores(here, m - 7, CAUSAL_KEYS, lambda: pe.wait_ge(k_normed.sem, here.at(k_normed, 2)))
                    if 0 <= m - 8 < HEADS:
                        turn_weights(here, m - 8, CAUSAL_KEYS)
                    if 0 <= m - 9 < HEADS:
                        weigh_values(here, m - 9, CAUSAL_KEYS)
                ffn(here, FFN_CHUNKS + MIX1, 1, norm_start(2, FFN_CHUNKS + MIX1), in_hi, in_lo, gate_act, prod_ready)

            with pe.Fori(0, DEPTH) as layer:
                here = Place(1, layer)

                def mean(n):
                    pe.wait_ge(z_sum.sem, here.at(z_sum, 2 * n + 2))
                    for f in range(2):
                        pe.matmul(banks[6][:, 0, :], mean_of, z_pairs[:, f, :], start=f == 0, stop=False)
                    pe.wait_ge(z_ready.sem, here.at(z_ready, HALVES * (n + 1)))
                    for f in (DT - 2, DT - 1):
                        e = pe.matmul(banks[6][:, 0, :], mean_of, x[:, f, :], start=False, stop=f == DT - 1)
                    e.then_inc(mu_ready.sem, 1)

                def variance(n):
                    for f in range(DT):
                        pe.wait_ge(c_sq.sem, here.at(c_sq, DT * n + f + 1))
                        for a in range(TT):
                            e = pe.matmul(banks[7][:, 0, a:a + 1], work[:, f, a * P:(a + 1) * P], mean_of[:, 0:1],
                                          start=f == 0 and a == 0, stop=f == DT - 1, skip_group_check=True)
                    e.then_inc(var_ready.sem, 1)

                def ln_factor(n):
                    pe.wait_ge(ln_rs.sem, here.at(ln_rs, n + 1))
                    spread_factor(rstd_ln).then_inc(ln_rstd.sem, 1)

                def settled(n):
                    def wait(k):
                        if n < 0:
                            pe.wait_ge(xg_ready.sem, xg_ready.before[1] - DT + k + 1)
                        pe.wait_ge(xs_ready.sem, here.at(xs_ready, DT * n + k + 1))
                    return wait

                for m in range(MIX2):
                    bank = banks[4 + m % 2]
                    take(here, m)
                    if 2 <= m < 22:
                        pe.wait_ge(mix_evac.sem, here.at(mix_evac, m - 1))
                    elif m == 22:
                        pe.wait_ge(ret_o.sem, here.at(ret_o, RET_HEADS))
                    elif m in (24, 25):
                        pe.wait_ge(mix_evac.sem, here.at(mix_evac, m - 3))
                    elif m == 28:
                        pe.wait_ge(branch_evac.sem, here.at(branch_evac, 1))
                        pe.wait_ge(ret_ready.sem, here.at(ret_ready, RET_HEADS))
                    elif m in (26, 27):
                        pe.wait_ge(mix_evac.sem, here.at(mix_evac, m - 3))
                    elif m in (30, 31, 32):
                        pe.wait_ge(branch_evac.sem, here.at(branch_evac, m - 27))
                    elif m == 36:
                        pe.wait_ge(mix_evac.sem, here.at(mix_evac, 26))
                        pe.wait_ge(ple_split.sem, here.at(ple_split, 1))
                    elif m in (38, 39):
                        pe.wait_ge(mix_evac.sem, here.at(mix_evac, 27))
                    elif m in (40, 41):
                        pe.wait_ge(mix_evac.sem, here.at(mix_evac, m - 11))
                    if m == 0:
                        features(m, two(bank), br_hi, br_lo, DT, k_first=settled(-1))
                    elif m in (4, 5) or 10 <= m < 14:
                        tokens(m, bank, br_hi, br_lo)
                    elif m in (22, 23):
                        at = 2 * (m - 22)
                        if m == 22:
                            pe.wait_ge(att_ready.sem, here.at(att_ready, HALVES))
                        features(m, two(banks[at]) + two(banks[at + 1]), att_hi, att_lo, HALVES)
                    elif 28 <= m < 32:
                        features(m, two(banks[m % 2]), in_hi, in_lo, DT)
                    elif 32 <= m < 36:
                        features(m, two(banks[m - 32]), br_hi, br_lo, DT, k_first=None if m > 32 else lambda k: pe.wait_ge(
                            merged_lo.sem, here.at(merged_lo, k // 2 + 1)))
                        if m == 35:
                            mean(0)
                    elif m in (36, 37):
                        at = 4 if m == 36 else 2
                        outs = two(banks[at]) + two(banks[at + 1])
                        if m == 36:
                            features(m, outs, ple_hi, ple_lo, 2)
                            variance(0)
                        else:
                            features(m, outs, ple_hi, ple_lo, 2, k_first=lambda k: ln_factor(0) if k == 1 else None)
                    elif m == 38:
                        features(m, two(bank), br_hi, br_lo, DT, k_first=settled(0))
                    else:
                        features(m, two(bank), br_hi, br_lo, DT)
                    if 0 <= m - 5 < HEADS:
                        scores(here, m - 5, ALL_KEYS, lambda: pe.wait_ge(mix_evac.sem, here.at(mix_evac, 4)))
                    if 0 <= m - 6 < HEADS:
                        turn_weights(here, m - 6, ALL_KEYS)
                    if 0 <= m - 7 < HEADS:
                        weigh_values(here, m - 7, ALL_KEYS)
                    if 0 <= m - 15 < RET_HEADS:
                        h = m - 15
                        pe.wait_ge(qk_ready.sem, here.at(qk_ready, 4))
                        if h >= 2:
                            pe.wait_ge(ret_p.sem, here.at(ret_p, h - 1))
                        for a in range(TT):
                            e = pe.matmul(banks[2 + h % 2][:, a, :], ret_qk[:, RET_HEADS + h, a * P:(a + 1) * P],
                                          ret_qk[:, h, :], start=True, stop=True, skip_group_check=True)
                        e.then_inc(ret_scored.sem, 1)
                    if 0 <= m - 16 < RET_HEADS:
                        h = m - 16
                        pe.wait_ge(ret_p.sem, here.at(ret_p, h + 1))
                        if h >= 2:
                            pe.wait_ge(ret_o.sem, here.at(ret_o, h - 1))
                        for a in range(TT):
                            for k in range(TT):
                                e = pe.matmul(banks[h % 2][:, a, :], softT[:, h % 2, k, a * P:(a + 1) * P],
                                              ret_v[:, k, h * RET_V:(h + 1) * RET_V], start=k == 0, stop=k == TT - 1,
                                              skip_group_check=True)
                        e.then_inc(ret_pv.sem, 1)
                    if 0 <= m - 18 < RET_HEADS:
                        h = m - 18
                        pe.wait_ge(ret_o.sem, here.at(ret_o, h + 1))
                        if h >= 1:
                            pe.wait_ge(ret_y.sem, here.at(ret_y, h))
                        for f in range(2):
                            for a in range(TT):
                                e = pe.transpose(banks[6][:, f, a * P:(a + 1) * P], soft[:, h % 2, a, f * P:(f + 1) * P], ident)
                        e.then_inc(ret_turned.sem, 1)

                def up_start(c):
                    if c < MIX2 + 2:
                        pe.wait_ge(mix_evac.sem, here.at(mix_evac, 31 + c - MIX2))
                        features(c, two(banks[4 + c - MIX2]), br_hi, br_lo, DT)
                    return c < MIX2 + 2
                ffn(here, MIX2, 0, up_start, br_hi, br_lo, gate_taps, up_taps)
                mean(1)
                variance(1)
                ln_factor(1)
    return nc


def _constants():
    f32 = np.float32
    k = np.zeros((P, CONSTS), f32)
    k[:, K_IDENT:K_IDENT + P] = np.eye(P)
    k[:, K_MEAN:K_MEAN + P] = 1.0 / D
    p = np.arange(P)
    k[:, K_HEAD:K_HEAD + P] = (p[:, None] // HEAD_DIM == p[None, :] // HEAD_DIM) / HEAD_DIM
    t = np.arange(T, dtype=f32)
    for half, cos, sin in ((TURN[0], K_COS1, K_SIN1), (TURN[1], K_COS2, K_SIN2)):
        low = p % (2 * half) < half
        j = np.arange(half, dtype=f32)
        if half == HEAD_DIM // 2:
            inv = (f32(1.0) / (f32(ROPE_BASE) ** (j * f32(2.0 / HEAD_DIM)))).astype(f32)
        else:
            inv = (f32(ROPE_BASE) ** (-j / f32(half))).astype(f32)
        angle = (t[None, :] * inv[p % half][:, None]).astype(f32).astype(np.float64)
        k[:, cos:cos + T] = np.cos(angle)
        k[:, sin:sin + T] = np.sin(angle) * np.where(low, -1.0, 1.0)[:, None]
    for a in range(TT):
        query = a * P + p[:, None]
        k[:, K_CAUSAL + a * T:K_CAUSAL + (a + 1) * T] = np.where(np.arange(T)[None, :] <= query, 0.0, NEG)
        dist = np.arange(T)[None, :] - query
        k[:, K_DIST + a * T:K_DIST + (a + 1) * T] = np.maximum(dist, 0)
        k[:, K_DIST + (TT + a) * T:K_DIST + (TT + a + 1) * T] = np.minimum(dist, 0)
    col = p % GRID_W
    start = np.clip(col - NA_COLS // 2, 0, GRID_W - NA_COLS)[:, None]
    key = np.arange(GRID_W)[None, :]
    k[:, K_WIN:K_WIN + GRID_W] = np.where((key >= start) & (key < start + NA_COLS), 0.0, NEG)
    for g, w in enumerate(WINDOWS):
        n = np.arange(POOL_EDGE)
        k[:, K_EDGE + g * POOL_EDGE:K_EDGE + (g + 1) * POOL_EDGE] = w / np.minimum(n + 1, w)
    return k


def _tile(w, rows, cols):
    part = w[rows, cols]
    return part.reshape(-1, P, part.shape[1]).transpose(1, 0, 2).reshape(P, -1)


def _ffn_chunks(up, down):
    whole = slice(None)

    def piece(kind, i):
        if kind == "D":
            return _tile(down, slice(i * T, (i + 1) * T), whole)
        at = i * T + (D_FF if kind == "B" else 0)
        return _tile(up, whole, slice(at, at + T))

    order = [("A", 0), ("B", 0)]
    for i in range(1, PAIRS):
        order += [("A", i), ("B", i), ("D", i - 1)]
    return [piece(*o) for o in order + [("D", PAIRS - 1)]]


def _columns(w, n, first=0):
    return [_tile(w, slice(None), slice(first + i * T, first + (i + 1) * T)) for i in range(n)]


def _stream(a):
    chunks = []
    for l in range(DEPTH):
        w, wide = a["w_in"][l], 4 * P
        chunks += _ffn_chunks(a["ffn1_w_gate_up"][l], a["ffn1_w_down"][l])
        chunks += _columns(w, 6, 512) + _columns(w, 2) + _columns(w, 8, 2048)
        chunks += [_tile(a["w_branch_pool"][l], slice(None), slice(i * wide, (i + 1) * wide)) for i in range(2)]
        chunks += [_tile(a["w_branch_attn"][l], slice(None), slice(i * wide, (i + 1) * wide)) for i in range(2)]
        chunks += _columns(a["w_out"][l], 4)
        chunks += _ffn_chunks(a["ffn2_w_gate_up"][l], a["ffn2_w_down"][l])
    for l in range(DEPTH):
        w = a["w_in_2"][l]
        chunks += _columns(w, 22)
        chunks += [_tile(a["w_branch_a_2"][l], slice(None), slice(i * wide, (i + 1) * wide)) for i in range(2)]
        chunks += _columns(w, 4, 22 * T)
        chunks += _columns(a["w_branch_b_2"][l], 4) + _columns(a["w_out_2"][l], 4)
        for i in range(2):
            half = np.zeros((P, CHUNK), np.float32)
            half[:, :CHUNK // 2] = _tile(a["w_ple_proj_2"][l], slice(None), slice(i * wide, (i + 1) * wide))
            chunks.append(half)
        chunks += _columns(a["w_ple_gate_2"][l], 4)
        chunks += _ffn_chunks(a["w_up_2"][l], a["w_down_2"][l])
    out = np.empty((STREAM, P, CHUNK), np.float32)
    for n, c in enumerate(chunks):
        out[n] = c
    assert len(chunks) == STREAM
    return out


def _col(v):
    return v.reshape(-1, P).T


def kernel(**inputs):
    import concourse.bacc as bacc
    from concourse.bass_utils import run_bass_kernel_spmd

    a = {k: np.ascontiguousarray(v) for k, v in inputs.items()}
    cols1 = np.concatenate([np.concatenate(
        [_col(a[n][l]) for n in ("ffn1_norm", "mix_norm", "ffn2_norm", "b_gate", "pool_scale")]
        + [np.concatenate([a[n][l], a[n][l]])[:, None] for n in ("q_norm", "k_norm")], axis=1)
        for l in range(DEPTH)] + [np.ones((P, COLS1), np.float32)], axis=1)
    cols2 = np.concatenate([np.concatenate(
        [_col(a[n][l]) for n in ("ln1_g_2", "ln1_b_2", "ln2_g_2", "ln2_b_2")]
        + [_col(a["conv_w_2"][l][tap]) for tap in range(3)] + [_col(a["conv_b_2"][l])]
        + [np.tile(a[n][l][None, :], (P, 1)) for n in ("ret_decay_f_2", "ret_decay_b_2")], axis=1)
        for l in range(DEPTH)], axis=1)
    q_row, q_col = (np.arange(P) // GRID_W)[:, None, None], (np.arange(P) % GRID_W)[:, None, None]
    step = np.arange(ROW_STEPS)[None, :, None] - (TT - 1) * (P // GRID_W)
    entry = (step - q_row + NA_ROWS - 1) * (2 * NA_COLS - 1) + np.arange(GRID_W)[None, None, :] - q_col + NA_COLS - 1
    rpb = a["na_rpb_2"].reshape(DEPTH, HEADS, -1)[:, :, entry].transpose(0, 2, 1, 3, 4).reshape(DEPTH, P, -1)
    arrays = {
        "xT": _tile(a["x"][0].T, slice(None), slice(None)),
        "stream": _stream(a),
        "cols1": cols1,
        "cols2": cols2,
        "pool_w": a["pool_w"].transpose(2, 0, 1, 3).reshape(P, -1),
        "pT": np.stack([_tile(a["p_2"][l, 0].T, slice(None), slice(None)) for l in range(DEPTH)]),
        "rpb": rpb,
        "consts": _constants(),
    }
    arrays = {k: np.ascontiguousarray(v) for k, v in arrays.items()}
    nc = bacc.Bacc("TRN2", target_bir_lowering=False, num_devices=1)
    args = [nc.dram_tensor(k, v.shape, F32, kind="ExternalInput").ap() for k, v in arrays.items()]
    args.append(nc.dram_tensor("result", (P, DT * T), F32, kind="ExternalOutput").ap())
    hybrid_and_neighbourhood_kernel(nc, *args)
    r = run_bass_kernel_spmd(nc, [arrays], core_ids=[0])
    got = r.results[0]["result"]
    return np.ascontiguousarray(got.reshape(P, DT, T).transpose(2, 1, 0).reshape(1, T, D))
```
